# Optimizing a Trainium2 kernel written in Bass

```python
import math
import jax, jax.numpy as jnp
from jax import lax
import numpy as np

D_MODEL = 2048
BATCH = 1
SEQ = 256
DEPTH = 1

CHUNK = 64
Q_BLOCK = 128
HEAD_DIM = 128
N_BRANCH = 4
BRANCH_WIDTH = D_MODEL // N_BRANCH
N_HEADS = BRANCH_WIDTH // HEAD_DIM
LRU_WIDTH = BRANCH_WIDTH
LRU_BLOCKS = N_HEADS
LRU_BLOCK = LRU_WIDTH // LRU_BLOCKS
CONV_WIDTH = 4
LRU_C = 8.0
LOOKBACK_CHUNKS = 8
BAND_CHUNKS = LOOKBACK_CHUNKS + 1
REL_CLIP = 256
REL_TABLE = REL_CLIP + CHUNK
D_FF = 4 * D_MODEL
ALPHA = (2.0 * DEPTH) ** 0.25
BETA = (8.0 * DEPTH) ** -0.25
LN_EPS = 1e-5

IN_SIZES = (
    BRANCH_WIDTH, BRANCH_WIDTH, BRANCH_WIDTH, N_HEADS,
    LRU_WIDTH, LRU_WIDTH,
    BRANCH_WIDTH, BRANCH_WIDTH, BRANCH_WIDTH,
    BRANCH_WIDTH, BRANCH_WIDTH, BRANCH_WIDTH,
)
D_IN = sum(IN_SIZES)

kernel_name = "chunk_causal_hybrid_fox_rglru_stickbreak_chunkattn"

F32 = jnp.float32

def layer_norm(x, g, b):
    xf = x.astype(F32)
    mu = jnp.mean(xf, axis=-1, keepdims=True)
    var = jnp.mean(jnp.square(xf - mu), axis=-1, keepdims=True)
    y = (xf - mu) * lax.rsqrt(var + LN_EPS) * g.astype(F32) + b.astype(F32)
    return y.astype(x.dtype)

def split_cols(u, sizes):
    outs, off = [], 0
    for n in sizes:
        outs.append(u[..., off:off + n])
        off += n
    return outs

def heads(t):
    b, s, _ = t.shape
    return t.reshape(b, s, N_HEADS, HEAD_DIM)

def fox_attention(q, k, v, f_logit):
    B, S, H, Dh = q.shape
    nb = S // Q_BLOCK
    cum_f = jnp.cumsum(jax.nn.log_sigmoid(f_logit.astype(F32)), axis=1)
    cum_f_k = cum_f.transpose(0, 2, 1)
    qb = q.reshape(B, nb, Q_BLOCK, H, Dh).transpose(1, 0, 2, 3, 4)
    fb = cum_f.reshape(B, nb, Q_BLOCK, H).transpose(1, 0, 3, 2)
    kpos = jnp.arange(S)
    scale = Dh ** -0.5

    def block(args):
        i, qi, fi = args
        s = jnp.einsum('bqhd,bkhd->bhqk', qi, k).astype(F32) * scale
        s = s + fi[..., :, None] - cum_f_k[:, :, None, :]
        qpos = i * Q_BLOCK + jnp.arange(Q_BLOCK)
        s = jnp.where(kpos[None, :] <= qpos[:, None], s, -jnp.inf)
        p = jax.nn.softmax(s, axis=-1)
        return jnp.einsum('bhqk,bkhd->bqhd', p.astype(v.dtype), v)

    out = lax.map(block, (jnp.arange(nb), qb, fb))
    return out.transpose(1, 0, 2, 3, 4).reshape(B, S, H * Dh)

def stick_breaking_attention(q, k, v):
    B, S, H, Dh = q.shape
    nb = S // Q_BLOCK
    qb = q.reshape(B, nb, Q_BLOCK, H, Dh).transpose(1, 0, 2, 3, 4)
    kpos = jnp.arange(S)
    scale = Dh ** -0.5

    def block(args):
        i, qi = args
        z = jnp.einsum('bqhd,bkhd->bhqk', qi, k).astype(F32) * scale
        qpos = i * Q_BLOCK + jnp.arange(Q_BLOCK)
        mask = kpos[None, :] < qpos[:, None]
        log_1m_beta = jnp.where(mask, jax.nn.log_sigmoid(-z), 0.0)
        later = lax.cumsum(log_1m_beta, axis=3, reverse=True) - log_1m_beta
        a = jnp.where(mask, jnp.exp(jax.nn.log_sigmoid(z) + later), 0.0)
        return jnp.einsum('bhqk,bkhd->bqhd', a.astype(v.dtype), v)

    out = lax.map(block, (jnp.arange(nb), qb))
    return out.transpose(1, 0, 2, 3, 4).reshape(B, S, H * Dh)

def chunk_band_attention(q, k, v, rel_bias):
    B, S, H, Dh = q.shape
    nc = S // CHUNK
    qc = q.reshape(B, nc, CHUNK, H, Dh)
    pad = ((0, 0), (LOOKBACK_CHUNKS, 0), (0, 0), (0, 0), (0, 0))
    kc = jnp.pad(k.reshape(B, nc, CHUNK, H, Dh), pad)
    vc = jnp.pad(v.reshape(B, nc, CHUNK, H, Dh), pad)
    kband = jnp.concatenate([kc[:, j:j + nc] for j in range(BAND_CHUNKS)], axis=2)
    vband = jnp.concatenate([vc[:, j:j + nc] for j in range(BAND_CHUNKS)], axis=2)
    kidx = jnp.arange(BAND_CHUNKS * CHUNK)
    dist = LOOKBACK_CHUNKS * CHUNK + jnp.arange(CHUNK)[:, None] - kidx[None, :]
    ridx = jnp.clip(dist, -(CHUNK - 1), REL_CLIP) + (CHUNK - 1)
    bias = rel_bias.astype(F32)[:, ridx]
    chunk_of_slot = jnp.arange(nc)[:, None] - LOOKBACK_CHUNKS + jnp.arange(BAND_CHUNKS)[None, :]
    valid = jnp.repeat(chunk_of_slot >= 0, CHUNK, axis=1)
    s = jnp.einsum('bcqhd,bckhd->bchqk', qc, kband).astype(F32) * (Dh ** -0.5)
    s = s + bias[None, None]
    s = jnp.where(valid[None, :, None, None, :], s, -jnp.inf)
    p = jax.nn.softmax(s, axis=-1)
    out = jnp.einsum('bchqk,bckhd->bcqhd', p.astype(v.dtype), vband)
    return out.reshape(B, S, H * Dh)

def recurrent_branch(xr, yr, conv_w, conv_b, w_r, b_r, w_i, b_i, lam):
    B, S, W = xr.shape
    xp = jnp.pad(xr, ((0, 0), (CONV_WIDTH - 1, 0), (0, 0)))
    xc = conv_b
    for j in range(CONV_WIDTH):
        xc = xc + xp[:, j:j + S] * conv_w[j]
    xg = xc.reshape(B, S, LRU_BLOCKS, LRU_BLOCK)
    r = jax.nn.sigmoid(jnp.einsum('bsnc,ncd->bsnd', xg, w_r).reshape(B, S, W) + b_r)
    gi = jax.nn.sigmoid(jnp.einsum('bsnc,ncd->bsnd', xg, w_i).reshape(B, S, W) + b_i)
    log_a = LRU_C * r.astype(F32) * jax.nn.log_sigmoid(lam.astype(F32))
    a = jnp.exp(log_a)
    inp = jnp.sqrt(-jnp.expm1(2.0 * log_a)) * (gi * xc).astype(F32)

    def combine(left, right):
        a1, b1 = left
        a2, b2 = right
        return a1 * a2, a2 * b1 + b2

    _, h = lax.associative_scan(combine, (a, inp), axis=1)
    return h.astype(xr.dtype) * jax.nn.gelu(yr)

def setup_inputs(seed: int = 0) -> dict:
    key = jax.random.key(seed)
    ks = jax.random.split(key, 24)
    L, D, Wb = DEPTH, D_MODEL, BRANCH_WIDTH

    def nrm(k, shape, scale):
        return jax.random.normal(k, shape, F32) * scale

    u = jax.random.uniform(ks[9], (L, LRU_WIDTH), F32, 0.9, 0.999)
    a0 = u ** (1.0 / LRU_C)
    lru_lambda = jnp.log(a0) - jnp.log1p(-a0)
    return {
        "x": nrm(ks[0], (BATCH, SEQ, D), 1.0),
        "ln_in_g": 1.0 + nrm(ks[1], (D,), 0.02),
        "ln_in_b": nrm(ks[2], (D,), 0.02),
        "w_in": nrm(ks[3], (L, D, D_IN), D ** -0.5),
        "b_forget": 3.0 + nrm(ks[4], (L, N_HEADS), 0.5),
        "conv_w": nrm(ks[5], (L, CONV_WIDTH, LRU_WIDTH), CONV_WIDTH ** -0.5),
        "conv_b": nrm(ks[6], (L, LRU_WIDTH), 0.02),
        "w_r": nrm(ks[7], (L, LRU_BLOCKS, LRU_BLOCK, LRU_BLOCK), LRU_BLOCK ** -0.5),
        "b_r": nrm(ks[8], (L, LRU_WIDTH), 0.02),
        "w_i": nrm(ks[10], (L, LRU_BLOCKS, LRU_BLOCK, LRU_BLOCK), LRU_BLOCK ** -0.5),
        "b_i": nrm(ks[11], (L, LRU_WIDTH), 0.02),
        "lru_lambda": lru_lambda,
        "rel_bias": nrm(ks[12], (L, N_HEADS, REL_TABLE), 0.1),
        "w_branch": nrm(ks[13], (L, N_BRANCH, Wb, D), Wb ** -0.5),
        "w_gate": nrm(ks[14], (L, N_BRANCH, D, D), D ** -0.5),
        "b_gate": nrm(ks[15], (L, N_BRANCH, D), 0.02),
        "w_out": nrm(ks[16], (L, D, D), BETA * D ** -0.5),
        "ln1_g": 1.0 + nrm(ks[17], (L, D), 0.02),
        "ln1_b": nrm(ks[18], (L, D), 0.02),
        "w_ff1": nrm(ks[19], (L, D, D_FF), D ** -0.5),
        "w_ff2": nrm(ks[20], (L, D_FF, D), BETA * D_FF ** -0.5),
        "ln2_g": 1.0 + nrm(ks[21], (L, D), 0.02),
        "ln2_b": nrm(ks[22], (L, D), 0.02),
    }

def reference(x, ln_in_g, ln_in_b, w_in, b_forget, conv_w, conv_b, w_r, b_r, w_i, b_i,
              lru_lambda, rel_bias, w_branch, w_gate, b_gate, w_out, ln1_g, ln1_b,
              w_ff1, w_ff2, ln2_g, ln2_b):
    x = layer_norm(x, ln_in_g, ln_in_b)
    for l in range(DEPTH):
        u = x @ w_in[l]
        (fq, fk, fv, ff, rx, ry, sq, sk, sv, cq, ck, cv) = split_cols(u, IN_SIZES)
        o_fox = fox_attention(heads(fq), heads(fk), heads(fv), ff + b_forget[l])
        o_lru = recurrent_branch(rx, ry, conv_w[l], conv_b[l], w_r[l], b_r[l],
                                 w_i[l], b_i[l], lru_lambda[l])
        o_sb = stick_breaking_attention(heads(sq), heads(sk), heads(sv))
        o_ch = chunk_band_attention(heads(cq), heads(ck), heads(cv), rel_bias[l])
        merged = None
        for g, o in enumerate((o_fox, o_lru, o_sb, o_ch)):
            gate = jax.nn.sigmoid(x @ w_gate[l, g] + b_gate[l, g])
            term = gate * (o @ w_branch[l, g])
            merged = term if merged is None else merged + term
        x = layer_norm(ALPHA * x + merged @ w_out[l], ln1_g[l], ln1_b[l])
        hid = jnp.square(jax.nn.relu(x @ w_ff1[l]))
        x = layer_norm(ALPHA * x + hid @ w_ff2[l], ln2_g[l], ln2_b[l])
    return x


_drawn_inputs = setup_inputs


def setup_inputs(seed=0):
    import zlib

    import numpy as np

    out = dict(_drawn_inputs(seed))
    spreads = {}
    factors = {'b_forget': 52.56,
     'conv_b': 4.052,
     'b_r': 64.0,
     'b_i': 59.357,
     'rel_bias': 8.0,
     'b_gate': 29.804,
     'ln1_g': 2.703,
     'ln1_b': 2.721,
     'ln2_g': 7.677,
     'ln2_b': 7.825}
    for name, (base, spread) in spreads.items():
        noise = np.random.default_rng([zlib.crc32(name.encode()), seed]).standard_normal(out[name].shape)
        drawn = base * np.exp(spread * noise) if base else spread * noise
        out[name] = __import__('jax').numpy.asarray(drawn.astype(out[name].dtype))
    for name, factor in factors.items():
        out[name] = (out[name] * factor).astype(out[name].dtype)
    return out
```

```python
from contextlib import ExitStack, contextmanager

import concourse.bass as bass
from concourse import mybir

F32 = mybir.dt.float32
F32R = mybir.dt.float32r
ALU = mybir.AluOpType
ACT = mybir.ActivationFunctionType
AX = mybir.AxisListType

P = 128
SEQ = 256
TT = SEQ // P
D = 2048
KT = D // P
NC = 512
CB = D // NC
HEADS = 4
CHUNK = 64
REL = 256 + CHUNK
CONV = 4
FF = 4 * D
SLAB_K = 2
SLABS = KT // SLAB_K
MIX_SLABS = NC // P // SLAB_K
RING = 4
LEAD = RING
IN_GROUPS = 11
QUARTERS = FF // D
GATE_STEPS = SLABS + MIX_SLABS
ROW_STEPS = 4 * GATE_STEPS
QUARTER_STEPS = 2 * CB * SLABS
ALPHA = 2.0 ** 0.25
SCALE = P ** -0.5
EPS = 1e-5
MASKED = -1e30
GELU_C = (2.0 / 3.141592653589793) ** 0.5
FOX, FORGET, LRU, STICK = 0, 3 * NC, 3 * NC + HEADS, 5 * NC + HEADS
LN_IN_G, LN_IN_B, LN1_G, LN1_B, CONV_W, CONV_B, B_R, B_I, LAM = 0, 16, 32, 48, 64, 80, 84, 88, 92
PARAMS = 96


class Count:

    def __init__(self, sem, start=0):
        self.sem, self.n, self.loops = sem, start, []

    def value(self, back=0):
        v = self.n - back
        for turn, per, _ in self.loops:
            v = turn * per + v
        return v

    def scaled(self, num, den):
        v = self.n // den * num
        for turn, per, _ in self.loops:
            assert per % den == 0
            v = turn * (per // den * num) + v
        return v

    def next(self, k=1):
        self.n += k
        return self.value()


@contextmanager
def loop(eng, trips, per):
    with eng.Fori(0, trips) as turn:
        for c, k in per.items():
            c.loops.append((turn, k, c.n))
        yield turn
        for c, k in per.items():
            _, _, start = c.loops.pop()
            assert c.n - start == k, (c.sem, c.n - start, k)
            c.n = start + k * trips


def build(nc, x, ln_in_g, ln_in_b, w_in, b_forget, conv_w, conv_b, w_r, b_r, w_i, b_i, lru_lambda,
          rel_bias, w_branch, w_gate, b_gate, w_out, ln1_g, ln1_b, w_ff1, w_ff2, ln2_g, ln2_b, out):
    with ExitStack() as ctx:
        top = [(nc.sbuf_base + 63) // 64 * 64]
        def place(name, shape, dtype=F32, at=None):
            size = 4
            for n in shape[1:]:
                size *= n
            if at is None:
                at = top[0]
                top[0] += (size + 63) // 64 * 64
            return nc.alloc_sbuf_tensor_at(name, shape, dtype, offset=at), at

        x_tok, _ = place("x_tok", [P, TT, D])
        xT_hi, _ = place("xT_hi", [P, KT, SEQ], F32R)
        xT_lo, _ = place("xT_lo", [P, KT, SEQ], F32R)
        zT_hi, z_at = place("zT_hi", [P, KT, SEQ], F32R)
        zT_lo, _ = place("zT_lo", [P, KT, SEQ], F32R)
        oT_hi, _ = place("oT_hi", [P, 4, HEADS, SEQ], F32R)
        oT_lo, _ = place("oT_lo", [P, 4, HEADS, SEQ], F32R)
        w_raw, _ = place("w_raw", [P, RING, SLAB_K, NC])
        w_hi, _ = place("w_hi", [P, RING, SLAB_K, NC], F32R)
        w_lo, _ = place("w_lo", [P, RING, SLAB_K, NC], F32R)
        stage, _ = place("stage", [P, TT, NC])
        gate, _ = place("gate", [P, TT, NC])
        b_gate_rows, _ = place("b_gate_rows", [P, 2, NC])
        qT, att_at = place("qT", [P, HEADS, SEQ])
        kT, _ = place("kT", [P, HEADS, SEQ])
        v_tok, v_at = place("v_tok", [P, TT, NC])
        logits, logits_at = place("logits", [P, 2, 3 * P])
        stick_l, _ = place("stick_l", [P, 3 * P])
        stick_b, _ = place("stick_b", [P, 3 * P])
        stick_c, _ = place("stick_c", [P, 3 * P])
        probsT, probsT_at = place("probsT", [P, 3 * P])
        fox_bias, bias_at = place("fox_bias", [P, HEADS, 3 * P])
        band_bias, _ = place("band_bias", [P, HEADS, SEQ], at=bias_at)
        lru = [place(f"lru_{c}", [P, HEADS, SEQ], at=z_at + 4096 * i)[0] for i, c in enumerate("abcdef")]
        w_ri, _ = place("w_ri", [P, 2, HEADS, P], at=v_at)
        forget_wide, _ = place("forget_wide", [P, TT, HEADS, P], at=logits_at)
        param_rows, _ = place("param_rows", [P, P], at=probsT_at)
        norm_rows, _ = place("norm_rows", [P, 2, D], at=att_at)
        ident, _ = place("ident", [P, P])
        upper, _ = place("upper", [P, SEQ])
        ones, _ = place("ones", [P, SEQ])
        causal_add, _ = place("causal_add", [P, P])
        strict_add, _ = place("strict_add", [P, P])
        strict_mul, _ = place("strict_mul", [P, P])
        params, _ = place("params", [P, PARAMS])
        wf_raw, _ = place("wf_raw", [P, KT, HEADS])
        wf_hi, _ = place("wf_hi", [P, KT, HEADS], F32R)
        wf_lo, _ = place("wf_lo", [P, KT, HEADS], F32R)
        bn, _ = place("bn", [P, TT, CB, 6])
        mean_var, _ = place("mean_var", [P, TT, 2])
        rstd, _ = place("rstd", [P, TT])
        peak, _ = place("peak", [P, 2])
        neg_peak, _ = place("neg_peak", [P, 2])
        total, _ = place("total", [P, 2])
        inv_total, _ = place("inv_total", [P, 2])
        b_forget_rows, _ = place("b_forget_rows", [P, TT, HEADS])
        sig, _ = place("sig", [P, 6, 12])
        cum_q, _ = place("cum_q", [P, TT, HEADS])
        lru_cols, _ = place("lru_cols", [P, 4, HEADS])
        assert top[0] <= nc.sbuf_usable_end, (top[0], nc.sbuf_usable_end)

        def psum(name):
            return ctx.enter_context(nc.psum_tensor(name, [P, NC], F32))
        acc = [[psum(f"acc{i}{t}") for t in range(TT)] for i in range(3)]
        aux = [psum("aux0"), psum("aux1")]

        def sem(name):
            return ctx.enter_context(nc.semaphore(name))
        x_loaded = [sem("x_loaded0"), sem("x_loaded1")]
        params_loaded = sem("params_loaded")
        small_loaded = sem("small_loaded")
        slab_loaded = [sem(f"slab_loaded{i}") for i in range(RING)]
        rel_loaded = sem("rel_loaded")
        gate_bias_loaded = [sem("gate_bias_loaded0"), sem("gate_bias_loaded1")]
        norm_loaded = sem("norm_loaded")
        norm_free = sem("norm_free")
        out_stored = sem("out_stored")
        consts_done = sem("consts_done")
        consts_ready = sem("consts_ready")
        hi_ready = sem("hi_ready")
        lo_ready = sem("lo_ready")
        slab_used = sem("slab_used")
        acc_taken = sem("acc_taken")
        aux_ready = [sem("aux_ready0"), sem("aux_ready1")]
        aux_taken = [sem("aux_taken0"), sem("aux_taken1")]
        var_ready = sem("var_ready")
        std_ready = sem("std_ready")
        xn_ready = sem("xn_ready")
        evac_hi = sem("evac_hi")
        wf_hi_ready = sem("wf_hi_ready")
        wf_ready = sem("wf_ready")
        u_taken = sem("u_taken")
        sig_in = sem("sig_in")
        sig_exp = sem("sig_exp")
        forget_ready = sem("forget_ready")
        conv_ready = sem("conv_ready")
        lru_cols_ready = sem("lru_cols_ready")
        gated_x_ready = sem("gated_x_ready")
        decay_exp_ready = sem("decay_exp_ready")
        decay_tanh_ready = sem("decay_tanh_ready")
        rest_ready = sem("rest_ready")
        root_ready = sem("root_ready")
        gelu_in_ready = sem("gelu_in_ready")
        gelu_tanh_ready = sem("gelu_tanh_ready")
        lru_out_ready = sem("lru_out_ready")
        branch_done = sem("branch_done")
        peak_ready = sem("peak_ready")
        exp_ready = sem("exp_ready")
        probs_ready = sem("probs_ready")
        stick_log_ready = sem("stick_log_ready")
        stick_logits_ready = sem("stick_logits_ready")
        rel_mask_ready = sem("rel_mask_ready")
        gate_in_ready = sem("gate_in_ready")
        gate_ready = sem("gate_ready")
        mix_taken = sem("mix_taken")
        merged_ready = sem("merged_ready")
        relu_ready = sem("relu_ready")
        residual_ready = sem("residual_ready")
        act_done = sem("act_done")
        dve_done = sem("dve_done")
        pool_done = sem("pool_done")
        y_ready = sem("y_ready")
        scaled_ready = sem("scaled_ready")

        block = ctx.enter_context(nc.Block())
        mark = {}

        @block.tensor
        def _(pe):
            slab = Count(slab_used)
            job = [Count(aux_taken[0]), Count(aux_taken[1])]
            projected = Count(u_taken)
            gated = Count(gate_in_ready)
            groups = Count(acc_taken)

            def free(b):
                if job[b].n:
                    pe.wait_ge(aux_taken[b], job[b].value())
                job[b].next()

            def start_projection():
                if projected.n >= 2:
                    pe.wait_ge(u_taken, projected.value(1))
                projected.next()

            def start_gate():
                if gated.n >= 2:
                    pe.wait_ge(gate_in_ready, gated.value(1))
                else:
                    pe.wait_ge(u_taken, IN_GROUPS - 1)
                gated.next()

            def start_group():
                if groups.n >= 2:
                    pe.wait_ge(acc_taken, groups.value(1))
                else:
                    pe.wait_ge(gate_in_ready, gated.value(1 - groups.n))
                groups.next()

            def products(pair, hi, lo, slabs, first, last):
                for s in slabs:
                    slot = slab.n % RING
                    slab.next()
                    pe.wait_ge(lo_ready, slab.value())
                    for kk in range(SLAB_K):
                        k = s * SLAB_K + kk
                        for t in range(TT):
                            toks = slice(t * P, (t + 1) * P)
                            begin = s == first and kk == 0
                            end = s == last and kk == SLAB_K - 1
                            nc.tensor.matmul(acc[pair][t][:], hi[:, k, toks], w_hi[:, slot, kk], start=begin, stop=False)
                            nc.tensor.matmul(acc[pair][t][:], lo[:, k, toks], w_hi[:, slot, kk], start=False, stop=False)
                            mm = nc.tensor.matmul(acc[pair][t][:], hi[:, k, toks], w_lo[:, slot, kk], start=False, stop=end)
                    mm.then_inc(slab_used, 1)

            def slabs_of(pair, hi, lo, slabs, total=SLABS):
                products(pair, hi, lo, slabs, 0, total - 1)

            def transpose_tokens(pair):
                b = pair % 2
                free(b)
                for kk in range(2):
                    k = 2 * pair + kk
                    for t in range(TT):
                        mm = nc.tensor.transpose(aux[b][:, kk * SEQ + t * P:kk * SEQ + (t + 1) * P],
                                                 x_tok[:, t, k * P:(k + 1) * P], ident[:])
                mm.then_inc(aux_ready[b], 1)

            def transpose_stage():
                for b in range(2):
                    free(b)
                    for kk in range(2):
                        k = 2 * b + kk
                        for t in range(TT):
                            mm = nc.tensor.transpose(aux[b][:, kk * SEQ + t * P:kk * SEQ + (t + 1) * P],
                                                     stage[:, t, k * P:(k + 1) * P], ident[:])
                    mm.then_inc(aux_ready[b], 1)

            def transpose_projected():
                pe.wait_ge(u_taken, projected.value(1))
                transpose_stage()

            def transpose_hidden(back):
                pe.wait_ge(acc_taken, groups.value(back))
                transpose_stage()

            pe.wait_ge(consts_ready, 1)
            pe.wait_ge(params_loaded, 16 * 9)
            free(0)
            nc.tensor.transpose(aux[0][:, 0:PARAMS], param_rows[0:PARAMS, :],
                                ident[0:PARAMS, 0:PARAMS]).then_inc(aux_ready[0], 1)
            pe.wait_ge(xn_ready, TT)
            transpose_tokens(0)
            transpose_tokens(1)
            start_projection()
            for s in range(SLABS):
                pe.wait_ge(aux_taken[s % 2], job[s % 2].value())
                slabs_of(0, xT_hi, xT_lo, [s])
                if s + 2 < SLABS:
                    transpose_tokens(s + 2)

            start_projection()
            slabs_of(1, xT_hi, xT_lo, [0])
            free(0)
            pe.wait_ge(wf_ready, 1)
            for t in range(TT):
                toks = slice(t * P, (t + 1) * P)
                for k in range(KT):
                    to = aux[0][:, t * HEADS:(t + 1) * HEADS]
                    nc.tensor.matmul(to, xT_hi[:, k, toks], wf_hi[:, k], start=k == 0, stop=False)
                    nc.tensor.matmul(to, xT_lo[:, k, toks], wf_hi[:, k], start=False, stop=False)
                    mm = nc.tensor.matmul(to, xT_hi[:, k, toks], wf_lo[:, k], start=False, stop=k == KT - 1)
            mm.then_inc(aux_ready[0], 1)
            slabs_of(1, xT_hi, xT_lo, [1, 2])
            transpose_projected()
            slabs_of(1, xT_hi, xT_lo, [3, 4])
            pe.wait_ge(forget_ready, 1)
            free(0)
            lf = forget_wide[:, :, :, 0]
            nc.tensor.matmul(aux[0][:, 0:HEADS], upper[:, 0:P], lf[:, 0], start=True, stop=True)
            nc.tensor.matmul(aux[0][:, HEADS:2 * HEADS], ones[:, 0:P], lf[:, 0], start=True, stop=False)
            nc.tensor.matmul(aux[0][:, HEADS:2 * HEADS], upper[:, 0:P], lf[:, 1],
                             start=False, stop=True).then_inc(aux_ready[0], 1)
            slabs_of(1, xT_hi, xT_lo, [5])
            for b in range(2):
                free(b)
                for hh in range(2):
                    h = 2 * b + hh
                    early = aux[b][:, hh * SEQ:hh * SEQ + P]
                    late = aux[b][:, hh * SEQ + P:(hh + 1) * SEQ]
                    nc.tensor.matmul(early, forget_wide[:, 0, h], upper[:, 0:P], start=True, stop=True)
                    nc.tensor.matmul(late, forget_wide[:, 0, h], upper[:, P:SEQ], start=True, stop=False)
                    mm = nc.tensor.matmul(late, forget_wide[:, 1, h], upper[:, 0:P], start=False, stop=True)
                mm.then_inc(aux_ready[b], 1)
            slabs_of(1, xT_hi, xT_lo, [6, 7])

            def recurrent_gate(which):
                for b in range(2):
                    free(b)
                    for hh in range(2):
                        n = 2 * b + hh
                        mm = nc.tensor.matmul(aux[b][:, hh * SEQ:(hh + 1) * SEQ], w_ri[:, which, n],
                                              lru[2][:, n, :], start=True, stop=True)
                    mm.then_inc(aux_ready[b], 1)

            start_projection()
            slabs_of(0, xT_hi, xT_lo, [0, 1, 2])
            transpose_projected()
            slabs_of(0, xT_hi, xT_lo, [3, 4])
            pe.wait_ge(conv_ready, 1)
            pe.wait_ge(small_loaded, 16 * 5)
            recurrent_gate(0)
            slabs_of(0, xT_hi, xT_lo, [5, 6])
            recurrent_gate(1)
            slabs_of(0, xT_hi, xT_lo, [7])
            for pair in (1, 2):
                start_projection()
                slabs_of(pair, xT_hi, xT_lo, [0, 1, 2])
                transpose_projected()
                slabs_of(pair, xT_hi, xT_lo, [3, 4, 5, 6, 7])

            ready = Count(probs_ready)
            values_back = [1]

            def scores(h):
                free(0)
                nc.tensor.matmul(aux[0][:, 0:P], qT[:, h, 0:P], kT[:, h, 0:P], start=True, stop=True)
                nc.tensor.matmul(aux[0][:, P:3 * P], qT[:, h, P:SEQ], kT[:, h, :],
                                 start=True, stop=True).then_inc(aux_ready[0], 1)

            def transpose_probs(h):
                pe.wait_ge(probs_ready, ready.next())
                free(1)
                p = logits[:, h % 2]
                for i in range(3):
                    mm = nc.tensor.transpose(aux[1][:, i * P:(i + 1) * P], p[:, i * P:(i + 1) * P], ident[:])
                mm.then_inc(aux_ready[1], 1)

            def mix(h):
                free(1)
                vh = slice(h * P, (h + 1) * P)
                nc.tensor.matmul(aux[1][:, 0:P], v_tok[:, 0, vh], probsT[:, 0:P], start=True, stop=True)
                nc.tensor.matmul(aux[1][:, P:SEQ], v_tok[:, 0, vh], probsT[:, P:SEQ], start=True, stop=False)
                nc.tensor.matmul(aux[1][:, P:SEQ], v_tok[:, 1, vh], probsT[:, SEQ:3 * P],
                                 start=False, stop=True).then_inc(aux_ready[1], 1)

            def attention_after(step):
                h = step // 3
                if step == 0:
                    pe.wait_ge(aux_taken[1], job[1].value())
                if step == 4:
                    pe.wait_ge(u_taken, projected.value(values_back[0]))
                if step % 3 == 0 and 1 <= h <= HEADS:
                    transpose_probs(h - 1)
                if step % 3 == 1 and 1 <= h <= HEADS:
                    mix(h - 1)
                if step % 3 == 0 and h < HEADS:
                    scores(h)

            per = {slab: 3 * SLABS, projected: 3, ready: HEADS, job[0]: HEADS + 2, job[1]: 2 * HEADS + 2}
            with loop(pe, 2, per):
                for pair in range(3):
                    start_projection()
                    for s in range(SLABS):
                        slabs_of(pair, xT_hi, xT_lo, [s])
                        step = pair * SLABS + s
                        attention_after(step)
                        if step in (14, 18):
                            transpose_projected()

            merged = Count(merged_ready)
            mixed = Count(mix_taken)

            def merge_row(first):
                for g in range(4):
                    start_gate()
                    for s in range(SLABS):
                        slabs_of(g % 2, xT_hi, xT_lo, [s])
                        step = g * GATE_STEPS + s
                        if first:
                            attention_after(step)
                        elif step == 2:
                            pe.wait_ge(merged_ready, merged.next())
                            transpose_stage()
                    if first and g == 0:
                        pe.wait_ge(u_taken, IN_GROUPS)
                    else:
                        pe.wait_ge(mix_taken, mixed.value())
                    if first:
                        if g == 1:
                            pe.wait_ge(branch_done, 1)
                        if g == 3:
                            pe.wait_ge(aux_taken[1], job[1].value())
                    mixed.next()
                    for s in range(MIX_SLABS):
                        products(2, oT_hi[:, g], oT_lo[:, g], [s], 0, MIX_SLABS - 1)
                        if first:
                            attention_after(g * GATE_STEPS + SLABS + s)

            values_back[0] = 0
            merge_row(True)
            mark["attention_done"] = job[1].n
            with loop(pe, CB - 1, {slab: ROW_STEPS, gated: 4, merged: 1, mixed: 4, job[0]: 1, job[1]: 1}):
                merge_row(False)

            for m in range(CB):
                start_group()
                if m == 0:
                    slabs_of(0, zT_hi, zT_lo, [0, 1, 2])
                    pe.wait_ge(merged_ready, merged.next())
                    transpose_stage()
                    slabs_of(0, zT_hi, zT_lo, [3, 4, 5])
                    for b in range(2):
                        pe.wait_ge(aux_taken[b], job[b].value())
                    slabs_of(0, zT_hi, zT_lo, [6, 7])
                else:
                    slabs_of(m % 2, zT_hi, zT_lo, range(SLABS))

            pe.wait_ge(xn_ready, 2 * TT)
            for pair in range(SLABS):
                transpose_tokens(pair)
            mark["x1_transposed"] = [job[0].n, job[1].n]
            for b in range(2):
                pe.wait_ge(aux_taken[b], job[b].value())

            with loop(pe, QUARTERS, {slab: QUARTER_STEPS, groups: 2 * CB, job[0]: CB, job[1]: CB}):
                for i in range(CB):
                    start_group()
                    slabs_of(i % 2, xT_hi, xT_lo, [0, 1, 2])
                    if i:
                        transpose_hidden(1)
                    slabs_of(i % 2, xT_hi, xT_lo, [3, 4, 5, 6, 7])
                for b in range(2):
                    pe.wait_ge(aux_taken[b], job[b].value())
                for i in range(CB):
                    start_group()
                    if i == 0:
                        slabs_of(0, zT_hi, zT_lo, [0, 1, 2])
                        transpose_hidden(1)
                        slabs_of(0, zT_hi, zT_lo, [3, 4, 5])
                        for b in range(2):
                            pe.wait_ge(aux_taken[b], job[b].value())
                        slabs_of(0, zT_hi, zT_lo, [6, 7])
                    else:
                        slabs_of(i % 2, zT_hi, zT_lo, range(SLABS))

        @block.scalar
        def _(act):
            slab = Count(hi_ready)
            job = [Count(aux_ready[0]), Count(aux_ready[1])]
            done = Count(act_done)
            std = Count(std_ready)
            hi_out = Count(evac_hi)

            def split(n):
                for _ in range(n):
                    slot = slab.n % RING
                    act.wait_ge(slab_loaded[slot], slab.scaled(16, RING) + 16)
                    if slab.n >= RING:
                        act.wait_ge(slab_used, slab.value(RING - 1))
                    nc.scalar.copy(w_hi[:, slot], w_raw[:, slot]).then_inc(hi_ready, 1)
                    slab.next()

            def settle():
                act.wait_ge(act_done, done.value())

            def did(ins):
                ins.then_inc(act_done, 1)
                done.next()

            def wait_job(b):
                act.wait_ge(aux_ready[b], job[b].next())

            def skip_job(b):
                job[b].next()

            def root(t):
                act.wait_ge(var_ready, std.next())
                nc.scalar.activation(rstd[:, t:t + 1], mean_var[:, t, 1:2], ACT.Sqrt).then_inc(std_ready, 1)

            def normed_pair(pair, gain, shift):
                b = pair % 2
                wait_job(b)
                for kk in range(2):
                    k = 2 * pair + kk
                    ins = nc.scalar.activation(xT_hi[:, k, :], aux[b][:, kk * SEQ:(kk + 1) * SEQ], ACT.Identity,
                                               scale=params[:, gain + k:gain + k + 1],
                                               bias=params[:, shift + k:shift + k + 1])
                    if kk == 0:
                        did(ins)
                ins.then_inc(evac_hi, 1)
                hi_out.next()

            rows = [(ln_in_g, LN_IN_G), (ln_in_b, LN_IN_B), (ln1_g[0], LN1_G), (ln1_b[0], LN1_B),
                    (conv_w[0].rearrange("j c -> (j c)"), CONV_W), (conv_b[0], CONV_B), (b_r[0], B_R),
                    (b_i[0], B_I), (lru_lambda[0], LAM)]
            for vec, at in rows:
                n = vec.shape[0] // P
                act.dma_start(param_rows[at:at + n, :], vec.rearrange("(k p) -> k p", p=P)).then_inc(params_loaded, 16)
            act.dma_start(wf_raw[:], w_in[0][:, FORGET:FORGET + HEADS].rearrange("(k p) n -> p k n", p=P)).then_inc(small_loaded, 16)
            act.dma_start(w_ri[:, 0], w_r[0].rearrange("n c d -> c n d")).then_inc(small_loaded, 16)
            act.dma_start(w_ri[:, 1], w_i[0].rearrange("n c d -> c n d")).then_inc(small_loaded, 16)
            for t in range(TT):
                act.dma_start(b_forget_rows[:, t, :], b_forget[0].partition_broadcast(P)).then_inc(small_loaded, 16)
            for t in range(TT):
                root(t)
            split(2)
            act.wait_ge(small_loaded, 16 * 5)
            nc.scalar.copy(wf_hi[:], wf_raw[:]).then_inc(wf_hi_ready, 1)
            split(2)
            skip_job(0)
            act.wait_ge(aux_taken[0], 1)
            normed_pair(0, LN_IN_G, LN_IN_B)
            normed_pair(1, LN_IN_G, LN_IN_B)
            for s in range(SLABS):
                split(1)
                if s + 2 < SLABS:
                    normed_pair(s + 2, LN_IN_G, LN_IN_B)

            def to_rows(rows, pair):
                act.wait_ge(slab_used, slab.value(LEAD))
                nc.scalar.copy(rows[:, 0, :], acc[pair][0][:])
                nc.scalar.copy(rows[:, 1, :], acc[pair][1][:]).then_inc(u_taken, 1)

            def from_stage(to):
                for b in range(2):
                    wait_job(b)
                    nc.scalar.copy(to[:, 2 * b:2 * b + 2, :],
                                   aux[b][:].rearrange("p (k t) -> p k t", k=2)).then_inc(aux_taken[b], 1)

            def recurrent_gate(to, which):
                for b in range(2):
                    wait_job(b)
                    for hh in range(2):
                        n = 2 * b + hh
                        ins = nc.scalar.activation(to[:, n, :], aux[b][:, hh * SEQ:(hh + 1) * SEQ], ACT.Tanh,
                                                   scale=0.5, bias=lru_cols[:, which, n:n + 1])
                    ins.then_inc(aux_taken[b], 1)

            def decay(to, func, which, signal):
                for n in range(HEADS):
                    c = lru_cols[:, which, n:n + 1]
                    ins = nc.scalar.activation(to[:, n, :], lru[3][:, n, :], func, scale=c, bias=c)
                ins.then_inc(signal, 1)

            a, b_, c_, d_, e_, f_ = lru
            to_rows(stage, 0)
            split(1)
            skip_job(0)
            act.wait_ge(sig_in, 1)
            nc.scalar.activation(sig[:, 2, :], sig[:, 1, :], ACT.Exp).then_inc(sig_exp, 1)
            split(2)
            from_stage(a)
            split(5)
            skip_job(0)
            skip_job(0)
            skip_job(1)
            to_rows(stage, 1)
            split(3)
            from_stage(b_)
            split(2)
            act.wait_ge(lru_cols_ready, 1)
            recurrent_gate(d_, 0)
            split(2)
            recurrent_gate(e_, 1)
            act.wait_ge(aux_taken[1], job[1].value())
            split(1)
            to_rows(stage, 0)
            split(1)
            decay(a, ACT.Exp, 2, decay_exp_ready)
            split(1)
            decay(f_, ACT.Tanh, 2, decay_tanh_ready)
            split(1)
            from_stage(qT)
            split(2)
            act.wait_ge(gated_x_ready, 1)
            decay(c_, ACT.Tanh, 3, decay_tanh_ready)
            split(3)
            to_rows(stage, 1)
            act.wait_ge(rest_ready, 1)
            nc.scalar.activation(f_[:], a[:], ACT.Sqrt, scale=-1.0).then_inc(root_ready, 1)
            split(3)
            from_stage(kT)
            split(1)
            act.wait_ge(gelu_in_ready, 1)
            nc.scalar.activation(f_[:], c_[:], ACT.Tanh, scale=GELU_C).then_inc(gelu_tanh_ready, 1)
            split(2)
            act.wait_ge(lru_out_ready, 1)
            nc.scalar.copy(oT_hi[:, 1], c_[:]).then_inc(evac_hi, 1)
            hi_out.next()
            split(2)
            to_rows(v_tok, 2)

            peaks = Count(peak_ready)
            stick = Count(stick_logits_ready)

            def probs_out(h):
                wait_job(1)
                nc.scalar.copy(probsT[:], aux[1][:, 0:3 * P]).then_inc(aux_taken[1], 1)

            def mixed_out(branch, h):
                wait_job(1)
                nc.scalar.copy(oT_hi[:, branch, h, :], aux[1][:, 0:SEQ]).then_inc(evac_hi, 1)
                hi_out.next()

            def softmax_exp(h):
                act.wait_ge(peak_ready, peaks.next())
                p = logits[:, h % 2]
                nc.scalar.activation(p[:, 0:P], p[:, 0:P], ACT.Exp, bias=neg_peak[:, 0:1], accum_out=total[:, 0:1])
                nc.scalar.activation(p[:, P:3 * P], p[:, P:3 * P], ACT.Exp, bias=neg_peak[:, 1:2],
                                     accum_out=total[:, 1:2]).then_inc(exp_ready, 1)

            def stick_log(h):
                wait_job(0)
                did(nc.scalar.activation(stick_l[:], aux[0][:, 0:3 * P], ACT.Abs, scale=SCALE))
                settle()
                did(nc.scalar.activation(stick_l[:], stick_l[:], ACT.Exp, scale=-1.0))
                settle()
                nc.scalar.activation(stick_l[:], stick_l[:], ACT.Ln, bias=1.0).then_inc(stick_log_ready, 1)

            def stick_exp(h):
                act.wait_ge(stick_logits_ready, stick.next())
                p = logits[:, h % 2]
                nc.scalar.activation(p, p, ACT.Exp).then_inc(probs_ready, 1)

            def attention_step(branch, step, stick_breaking):
                h = step // 3
                if step % 3 == 0:
                    if 1 <= h <= HEADS:
                        probs_out(h - 1)
                    if h < HEADS:
                        if stick_breaking:
                            stick_log(h)
                        else:
                            skip_job(0)
                if step % 3 == 1:
                    if 1 <= h <= HEADS:
                        mixed_out(branch, h - 1)
                    if h < HEADS and not stick_breaking:
                        softmax_exp(h)
                if step % 3 == 2 and h < HEADS and stick_breaking:
                    stick_exp(h)

            for branch in (0, 2):
                for step in range(3 * SLABS):
                    split(1)
                    attention_step(branch, step, branch == 2)
                    if step == 7:
                        to_rows(stage, 0)
                    if step == 14:
                        from_stage(qT)
                    if step == 15:
                        to_rows(stage, 1)
                    if step == 18:
                        from_stage(kT)
                    if step == 23:
                        to_rows(v_tok, 2)

            gates = Count(gate_in_ready)

            def halves_out(hi_to, b, scale=1.0):
                nc.scalar.activation(hi_to, aux[b][:].rearrange("p (k t) -> p k t", k=2), ACT.Copy,
                                     scale=scale).then_inc(evac_hi, 1)
                hi_out.next()

            def merge_row(first, n=None):
                for step in range(ROW_STEPS):
                    g, s = divmod(step, GATE_STEPS)
                    if not first and step == 3:
                        for b in range(2):
                            wait_job(b)
                    split(1)
                    if first:
                        attention_step(3, step, False)
                    elif step == 3:
                        for b in range(2):
                            k = n * (NC // P) + 2 * b
                            halves_out(zT_hi[:, bass.ds(k, 2), :], b, 0.5)
                    if s == SLABS:
                        act.wait_ge(gate_in_ready, gates.next())
                        nc.scalar.activation(gate[:], gate[:], ACT.Tanh, scale=0.5).then_inc(gate_ready, 1)

            merge_row(True)
            with loop(act, CB - 1, {slab: ROW_STEPS, job[0]: 1, job[1]: 1, hi_out: 2, gates: 4}) as n:
                merge_row(False, n)

            split(3)
            for b in range(2):
                wait_job(b)
                halves_out(zT_hi[:, (CB - 1) * (NC // P) + 2 * b:(CB - 1) * (NC // P) + 2 * b + 2, :], b, 0.5)
            split(CB * SLABS - 3)

            for t in range(TT):
                root(t)
            for pair in range(SLABS):
                normed_pair(pair, LN1_G, LN1_B)

            relus = Count(relu_ready)
            with loop(act, QUARTERS, {slab: QUARTER_STEPS, job[0]: CB, job[1]: CB, hi_out: 2 * CB, relus: CB}) as q:
                for step in range(QUARTER_STEPS - LEAD):
                    split(1)
                    i, s = divmod(step, SLABS)
                    if s == 2 and 1 <= i <= CB:
                        for b in range(2):
                            wait_job(b)
                            k = (i - 1) * (NC // P) + 2 * b
                            halves_out(zT_hi[:, k:k + 2, :], b)
                    if s == SLABS - 1 and i < CB:
                        act.wait_ge(slab_used, slab.value(LEAD))
                        nc.scalar.activation(stage[:, 0], acc[i % 2][0][:], ACT.Relu)
                        nc.scalar.activation(stage[:, 1], acc[i % 2][1][:], ACT.Relu).then_inc(relu_ready, 1)
                        relus.next()
                with act.If(QUARTERS - 1 - q):
                    split(LEAD)
            for t in range(TT):
                root(t)

        @block.vector
        def _(dve):
            slab = Count(lo_ready)
            job = [Count(aux_ready[0]), Count(aux_ready[1])]
            done = Count(dve_done)
            std = Count(std_ready)
            hi_in = Count(evac_hi)
            acc_done = Count(acc_taken)
            v = nc.vector

            def split(n):
                for _ in range(n):
                    slot = slab.n % RING
                    dve.wait_ge(hi_ready, slab.next())
                    v.tensor_sub(w_lo[:, slot], w_raw[:, slot], w_hi[:, slot]).then_inc(lo_ready, 1)

            def did(ins):
                ins.then_inc(dve_done, 1)
                done.next()

            def settle():
                dve.wait_ge(dve_done, done.value())

            def chain(ins):
                did(ins)
                settle()

            def wait_job(b):
                dve.wait_ge(aux_ready[b], job[b].next())

            def skip_job(b):
                job[b].next()

            def statistics(t, m):
                did(v.bn_stats(bn[:, t, m], x_tok[:, t, m * NC:(m + 1) * NC]))

            def spread(t):
                settle()
                chain(v.bn_aggr(mean_var[:, t], bn[:, t].rearrange("p m s -> p (m s)")))
                v.tensor_scalar(mean_var[:, t, 1:2], mean_var[:, t, 1:2], EPS, None, ALU.add).then_inc(var_ready, 1)

            def normalise(t):
                dve.wait_ge(std_ready, std.next())
                chain(v.reciprocal(rstd[:, t:t + 1], rstd[:, t:t + 1]))
                v.tensor_scalar(x_tok[:, t], x_tok[:, t], mean_var[:, t, 0:1], rstd[:, t:t + 1],
                                ALU.subtract, ALU.mult).then_inc(xn_ready, 1)

            def normed_pair(pair, gain, shift):
                b = pair % 2
                wait_job(b)
                dve.wait_ge(evac_hi, hi_in.next())
                for kk in range(2):
                    k = 2 * pair + kk
                    did(v.tensor_scalar(gate[:, b, kk * SEQ:(kk + 1) * SEQ], aux[b][:, kk * SEQ:(kk + 1) * SEQ],
                                        params[:, gain + k:gain + k + 1], params[:, shift + k:shift + k + 1],
                                        ALU.mult, ALU.add))
                settle()
                ks = slice(2 * pair, 2 * pair + 2)
                v.tensor_sub(xT_lo[:, ks], gate[:, b].rearrange("p (k t) -> p k t", k=2),
                             xT_hi[:, ks]).then_inc(aux_taken[b], 1)

            for t in range(TT):
                dve.wait_ge(x_loaded[t], 16)
                for m in range(CB):
                    statistics(t, m)
                spread(t)
                normalise(t)
            wait_job(0)
            v.tensor_copy(params[:], aux[0][:, 0:PARAMS]).then_inc(aux_taken[0], 1)
            split(2)
            dve.wait_ge(wf_hi_ready, 1)
            v.tensor_sub(wf_lo[:], wf_raw[:], wf_hi[:]).then_inc(wf_ready, 1)
            split(2)
            dve.wait_ge(aux_taken[0], 1)
            normed_pair(0, LN_IN_G, LN_IN_B)
            normed_pair(1, LN_IN_G, LN_IN_B)
            for s in range(SLABS):
                split(1)
                if s + 2 < SLABS:
                    normed_pair(s + 2, LN_IN_G, LN_IN_B)

            a, b_, c_, d_, e_, f_ = lru
            arg, neg, ex, s1, s2, acc_ = [sig[:, i] for i in range(6)]
            split(1)
            wait_job(0)
            did(v.tensor_copy(arg[:, 8:12], params[:, LAM:LAM + HEADS]))
            v.tensor_tensor(arg[:, 0:8], aux[0][:, 0:8], b_forget_rows[:].rearrange("p t h -> p (t h)"),
                            ALU.add).then_inc(aux_taken[0], 1)
            settle()
            dve.wait_ge(aux_taken[0], job[0].value())
            v.scalar_tensor_tensor(neg, arg, -1.0, arg, ALU.mult, ALU.min).then_inc(sig_in, 1)
            did(v.tensor_scalar(lru_cols[:, 0], params[:, B_R:B_R + HEADS], 0.5, None, ALU.mult))
            did(v.tensor_scalar(lru_cols[:, 1], params[:, B_I:B_I + HEADS], 0.5, None, ALU.mult))
            split(1)
            dve.wait_ge(sig_exp, 1)
            chain(v.tensor_scalar(s1, ex, 2.0, None, ALU.add))
            chain(v.reciprocal(s1, s1))
            chain(v.tensor_tensor(s1, s1, ex, ALU.mult))
            chain(v.tensor_tensor(s2, s1, s1, ALU.mult))
            chain(v.tensor_scalar(acc_, s2, 1.0 / 15, None, ALU.mult))
            for odd in (13, 11, 9, 7, 5, 3):
                chain(v.scalar_tensor_tensor(acc_, acc_, 1.0 / odd, s2, ALU.add, ALU.mult))
            chain(v.scalar_tensor_tensor(acc_, acc_, 1.0, s1, ALU.add, ALU.mult))
            chain(v.tensor_scalar(neg, arg, 0.0, None, ALU.min))
            chain(v.scalar_tensor_tensor(acc_, acc_, -2.0, neg, ALU.mult, ALU.add))
            did(v.tensor_scalar(lru_cols[:, 2], acc_[:, 8:12], 4.0, None, ALU.mult))
            v.tensor_scalar(lru_cols[:, 3], acc_[:, 8:12], 2.0, None, ALU.mult).then_inc(lru_cols_ready, 1)
            split(1)
            v.tensor_copy(forget_wide[:].rearrange("p t h c -> p (t h) c"),
                          acc_[:, 0:8].unsqueeze(2).to_broadcast([P, 8, P])).then_inc(forget_ready, 1)

            skip_job(0)
            skip_job(1)
            for n in range(HEADS):
                split(1)
                if n == 0:
                    dve.wait_ge(aux_taken[0], job[0].value())
                    dve.wait_ge(aux_taken[1], job[1].value())
                tap = [params[:, CONV_W + j * HEADS + n:CONV_W + j * HEADS + n + 1] for j in range(CONV)]
                chain(v.tensor_scalar(c_[:, n], a[:, n], tap[CONV - 1], params[:, CONV_B + n:CONV_B + n + 1],
                                      ALU.mult, ALU.add))
                for j in reversed(range(CONV - 1)):
                    lag = CONV - 1 - j
                    ins = v.scalar_tensor_tensor(c_[:, n, lag:], a[:, n, 0:SEQ - lag], tap[j], c_[:, n, lag:],
                                                 ALU.mult, ALU.add)
                    if j or n < HEADS - 1:
                        chain(ins)
                if n == 1:
                    wait_job(0)
                    v.tensor_copy(cum_q[:].rearrange("p t h -> p (t h)"), aux[0][:, 0:8]).then_inc(aux_taken[0], 1)
            ins.then_inc(conv_ready, 1)
            split(1)

            dve.wait_ge(aux_taken[0], job[0].value())
            for b in range(2):
                wait_job(b)
                for hh in range(2):
                    h = 2 * b + hh
                    sums = aux[b][:, hh * SEQ:(hh + 1) * SEQ]
                    did(v.tensor_scalar(fox_bias[:, h, 0:P], sums[:, 0:P], -1.0, cum_q[:, 0, h:h + 1], ALU.mult, ALU.add))
                    ins = v.tensor_scalar(fox_bias[:, h, P:3 * P], sums, -1.0, cum_q[:, 1, h:h + 1], ALU.mult, ALU.add)
                    if hh == 0:
                        did(ins)
                ins.then_inc(aux_taken[b], 1)
                dve.wait_ge(aux_taken[b], job[b].value())
                split(1)
            settle()
            diagonal = fox_bias[:].rearrange("p h (c k) -> p h c k", k=P)[:, :, 0::2, :]
            chain(v.tensor_tensor(diagonal, diagonal,
                                  causal_add[:].unsqueeze(1).unsqueeze(1).to_broadcast([P, HEADS, 2, P]), ALU.add))
            split(1)

            for _ in range(2):
                skip_job(0)
                skip_job(1)
            split(4)
            skip_job(0)
            skip_job(1)
            for b in range(2):
                dve.wait_ge(aux_taken[b], job[b].value())
            v.scalar_tensor_tensor(e_[:], e_[:], 1.0, c_[:], ALU.add, ALU.mult).then_inc(gated_x_ready, 1)
            split(6)
            dve.wait_ge(gated_x_ready, 1)
            dve.wait_ge(decay_exp_ready, 1)
            dve.wait_ge(decay_tanh_ready, 2)
            chain(v.scalar_tensor_tensor(c_[:], a[:], 1.0, c_[:], ALU.add, ALU.mult))
            chain(v.tensor_scalar(d_[:], c_[:], 1.0, None, ALU.add))
            split(1)
            chain(v.tensor_tensor(a[:], d_[:], d_[:], ALU.mult))
            v.scalar_tensor_tensor(a[:], a[:], 1.0, f_[:], ALU.add, ALU.mult).then_inc(rest_ready, 1)
            split(1)
            chain(v.tensor_tensor(c_[:], b_[:], b_[:], ALU.mult))
            split(1)
            chain(v.tensor_scalar(c_[:], c_[:], 0.044715, 1.0, ALU.mult, ALU.add))
            chain(v.tensor_tensor(c_[:], c_[:], b_[:], ALU.mult))
            split(1)
            dve.wait_ge(root_ready, 1)
            v.scalar_tensor_tensor(e_[:], e_[:], 0.5, f_[:], ALU.mult, ALU.mult).then_inc(gelu_in_ready, 1)
            dve.wait_ge(gelu_in_ready, 1)
            dve.wait_ge(rest_ready, 1)
            split(1)
            for n in range(HEADS):
                did(v.tensor_tensor_scan(a[:, n], d_[:, n], e_[:, n], 0.0, ALU.mult, ALU.add))
                if n == 1:
                    split(1)
            settle()
            split(1)
            dve.wait_ge(gelu_tanh_ready, 1)
            chain(v.scalar_tensor_tensor(c_[:], f_[:], 1.0, b_[:], ALU.add, ALU.mult))
            v.scalar_tensor_tensor(c_[:], c_[:], 0.5, a[:], ALU.mult, ALU.mult).then_inc(lru_out_ready, 1)
            split(2)
            dve.wait_ge(lru_out_ready, 1)
            dve.wait_ge(evac_hi, hi_in.next())
            v.tensor_sub(oT_lo[:, 1], c_[:], oT_hi[:, 1]).then_inc(branch_done, 1)
            split(2)
            for _ in range(2):
                skip_job(0)
                skip_job(1)

            exps = Count(exp_ready)
            logs = Count(stick_log_ready)

            def softmax_logits(h, bias0, bias1):
                wait_job(0)
                p = logits[:, h % 2]
                did(v.scalar_tensor_tensor(p[:, 0:P], aux[0][:, 0:P], SCALE, bias0, ALU.mult, ALU.add))
                v.scalar_tensor_tensor(p[:, P:3 * P], aux[0][:, P:3 * P], SCALE, bias1,
                                       ALU.mult, ALU.add).then_inc(aux_taken[0], 1)
                settle()
                dve.wait_ge(aux_taken[0], job[0].value())
                did(v.tensor_reduce(peak[:, 0:1], p[:, 0:P], AX.X, ALU.max))
                chain(v.tensor_reduce(peak[:, 1:2], p[:, P:3 * P], AX.X, ALU.max))
                v.tensor_scalar(neg_peak[:], peak[:], -1.0, None, ALU.mult).then_inc(peak_ready, 1)

            def softmax_scale(h):
                dve.wait_ge(exp_ready, exps.next())
                p = logits[:, h % 2]
                chain(v.reciprocal(inv_total[:], total[:]))
                did(v.tensor_scalar(p[:, 0:P], p[:, 0:P], inv_total[:, 0:1], None, ALU.mult))
                v.tensor_scalar(p[:, P:3 * P], p[:, P:3 * P], inv_total[:, 1:2], None, ALU.mult).then_inc(probs_ready, 1)

            def stick_relu(h):
                wait_job(0)
                dve.wait_ge(stick_log_ready, logs.next())
                chain(v.tensor_scalar(stick_b[:], aux[0][:, 0:3 * P], SCALE, 0.0, ALU.mult, ALU.max))

            def stick_logits(h):
                chain(v.scalar_tensor_tensor(stick_b[:], stick_b[:], -1.0, stick_l[:], ALU.mult, ALU.subtract))
                diag = stick_b[:].rearrange("p (c k) -> p c k", k=P)[:, 0::2, :]
                chain(v.tensor_tensor(diag, diag, strict_mul[:].unsqueeze(1).to_broadcast([P, 2, P]), ALU.mult))
                did(v.tensor_tensor_scan(stick_c[:, P - 1::-1], ones[:, 0:P], stick_b[:, P - 1::-1], 0.0, ALU.mult, ALU.add))
                chain(v.tensor_tensor_scan(stick_c[:, 3 * P - 1:P - 1:-1], ones[:], stick_b[:, 3 * P - 1:P - 1:-1],
                                           0.0, ALU.mult, ALU.add))
                p = logits[:, h % 2]
                v.scalar_tensor_tensor(p, aux[0][:, 0:3 * P], SCALE, stick_c[:], ALU.mult, ALU.add).then_inc(aux_taken[0], 1)
                dve.wait_ge(aux_taken[0], job[0].value())
                diag = p.rearrange("p (c k) -> p c k", k=P)[:, 0::2, :]
                v.tensor_tensor(diag, diag, strict_add[:].unsqueeze(1).to_broadcast([P, 2, P]),
                                ALU.add).then_inc(stick_logits_ready, 1)

            def mixed_out(branch, h):
                wait_job(1)
                dve.wait_ge(evac_hi, hi_in.next())
                v.tensor_sub(oT_lo[:, branch, h, :], aux[1][:, 0:SEQ], oT_hi[:, branch, h, :]).then_inc(aux_taken[1], 1)

            def attention_step(branch, step):
                h = step // 3
                if step % 3 == 0 and 1 <= h <= HEADS:
                    skip_job(1)
                if step % 3 == 1 and 1 <= h <= HEADS:
                    mixed_out(branch, h - 1)
                if h >= HEADS:
                    return
                if branch == 2:
                    if step % 3 == 1:
                        stick_relu(h)
                        stick_logits(h)
                else:
                    if step % 3 == 0 and branch == 0:
                        softmax_logits(h, fox_bias[:, h, 0:P], fox_bias[:, h, P:3 * P])
                    if step % 3 == 0 and branch == 3:
                        softmax_logits(h, band_bias[:, h, P - 1::-1], band_bias[:, h, SEQ - 1::-1])
                    if step % 3 == 2:
                        softmax_scale(h)

            for branch in (0, 2):
                for step in range(3 * SLABS):
                    split(1)
                    attention_step(branch, step)
                    if step in (14, 18):
                        skip_job(0)
                        skip_job(1)
                    if branch == 0 and step == 11:
                        v.memset(band_bias[0:CHUNK, :, 0:CHUNK], MASKED).then_inc(rel_mask_ready, 1)

            gates = Count(gate_ready)
            biases = Count(gate_bias_loaded[0])

            def merge_row(first, n=None):
                for step in range(ROW_STEPS):
                    g, s = divmod(step, GATE_STEPS)
                    split(1)
                    if first:
                        if step == 0:
                            dve.wait_ge(rel_loaded, 32)
                            dve.wait_ge(rel_mask_ready, 1)
                        attention_step(3, step)
                    elif step == 2:
                        for b in range(2):
                            wait_job(b)
                            dve.wait_ge(evac_hi, hi_in.next())
                            k = n * (NC // P) + 2 * b
                            v.scalar_tensor_tensor(zT_lo[:, bass.ds(k, 2), :], aux[b][:].rearrange("p (k t) -> p k t", k=2),
                                                   0.5, zT_hi[:, bass.ds(k, 2), :], ALU.mult, ALU.subtract).then_inc(aux_taken[b], 1)
                    if s == SLABS - 1:
                        dve.wait_ge(slab_used, slab.value(LEAD))
                        dve.wait_ge(gate_bias_loaded[g % 2], biases.scaled(16, 2) + 16)
                        biases.next()
                        v.tensor_tensor(gate[:, 0], acc[g % 2][0][:], b_gate_rows[:, g % 2], ALU.add)
                        v.tensor_tensor(gate[:, 1], acc[g % 2][1][:], b_gate_rows[:, g % 2], ALU.add).then_inc(gate_in_ready, 1)
                    if s == GATE_STEPS - 1:
                        dve.wait_ge(slab_used, slab.value(LEAD))
                        dve.wait_ge(gate_ready, gates.next())
                        for t in range(TT):
                            to = stage if g == 0 else gate
                            ins = v.scalar_tensor_tensor(to[:, t], gate[:, t], 1.0, acc[2][t][:], ALU.add, ALU.mult)
                        ins.then_inc(mix_taken, 1)
                        mixed.next()
                        if g:
                            dve.wait_ge(mix_taken, mixed.value())
                            ins = v.tensor_tensor(stage[:], stage[:], gate[:], ALU.add)
                            if g == 3:
                                ins.then_inc(merged_ready, 1)
                            else:
                                did(ins)
                                settle()

            mixed = Count(mix_taken)
            merge_row(True)
            with loop(dve, CB - 1, {slab: ROW_STEPS, job[0]: 1, job[1]: 1, hi_in: 2, gates: 4, biases: 4,
                                    mixed: 4, done: 2}) as n:
                merge_row(False, n)

            split(3)
            for b in range(2):
                wait_job(b)
                dve.wait_ge(evac_hi, hi_in.next())
                k = (CB - 1) * (NC // P) + 2 * b
                v.scalar_tensor_tensor(zT_lo[:, k:k + 2, :], aux[b][:].rearrange("p (k t) -> p k t", k=2),
                                       0.5, zT_hi[:, k:k + 2, :], ALU.mult, ALU.subtract).then_inc(aux_taken[b], 1)
            for m in range(CB):
                split(SLABS - 3 if m == 0 else SLABS)
                dve.wait_ge(slab_used, slab.value(LEAD))
                if m == 0:
                    dve.wait_ge(residual_ready, 1)
                cols = slice(m * NC, (m + 1) * NC)
                for t in range(TT):
                    ins = v.scalar_tensor_tensor(x_tok[:, t, cols], x_tok[:, t, cols], ALPHA, acc[m % 2][t][:], ALU.mult, ALU.add)
                ins.then_inc(acc_taken, 1)
                acc_done.next()
                dve.wait_ge(acc_taken, acc_done.value())
                for t in range(TT):
                    statistics(t, m)
            for t in range(TT):
                spread(t)
                normalise(t)
            for pair in range(SLABS):
                normed_pair(pair, LN1_G, LN1_B)

            relus = Count(relu_ready)
            dve.wait_ge(residual_ready, 2)
            with loop(dve, QUARTERS, {relus: CB, slab: QUARTER_STEPS, job[0]: CB, job[1]: CB, hi_in: 2 * CB,
                                      acc_done: 2 * CB, done: 2 * CB}) as q:
                for step in range(QUARTER_STEPS):
                    if step < QUARTER_STEPS - LEAD:
                        split(1)
                    elif step == QUARTER_STEPS - LEAD:
                        with dve.If(QUARTERS - 1 - q):
                            split(LEAD)
                    i, s = divmod(step, SLABS)
                    if s == 2 and 1 <= i <= CB:
                        for b in range(2):
                            wait_job(b)
                            dve.wait_ge(evac_hi, hi_in.next())
                            k = (i - 1) * (NC // P) + 2 * b
                            v.tensor_sub(zT_lo[:, k:k + 2, :], aux[b][:].rearrange("p (k t) -> p k t", k=2),
                                         zT_hi[:, k:k + 2, :]).then_inc(aux_taken[b], 1)
                    if s == SLABS - 1:
                        dve.wait_ge(slab_used, slab.value(LEAD))
                        if i < CB:
                            dve.wait_ge(relu_ready, relus.next())
                        for t in range(TT):
                            if i < CB:
                                ins = v.tensor_tensor(stage[:, t], acc[i % 2][t][:], stage[:, t], ALU.mult)
                            else:
                                m = i - CB
                                cols = slice(m * NC, (m + 1) * NC)
                                ins = v.tensor_tensor(x_tok[:, t, cols], x_tok[:, t, cols], acc[i % 2][t][:], ALU.add)
                        ins.then_inc(acc_taken, 1)
                        acc_done.next()
                        if i >= CB:
                            dve.wait_ge(acc_taken, acc_done.value())
                            for t in range(TT):
                                statistics(t, i - CB)

            for t in range(TT):
                spread(t)
            dve.wait_ge(norm_loaded, 96)
            for t in range(TT):
                dve.wait_ge(std_ready, std.next())
                chain(v.reciprocal(rstd[:, t:t + 1], rstd[:, t:t + 1]))
                for m in range(CB):
                    cols = slice(m * NC, (m + 1) * NC)
                    chain(v.tensor_scalar(x_tok[:, t, cols], x_tok[:, t, cols], mean_var[:, t, 0:1],
                                          rstd[:, t:t + 1], ALU.subtract, ALU.mult))
                    v.tensor_tensor(x_tok[:, t, cols], x_tok[:, t, cols], norm_rows[:, 0, cols],
                                    ALU.mult).then_inc(scaled_ready, 1)

        @block.gpsimd
        def _(pool):
            g = nc.gpsimd
            for tile, value in ((ident, 0.0), (upper, 1.0), (ones, 1.0), (causal_add, 0.0), (strict_add, 0.0),
                                (strict_mul, 1.0)):
                ins = g.memset(tile[:], value)
            ins.then_inc(pool_done, 1)
            pool.wait_ge(pool_done, 1)
            g.affine_select(out=ident[:], in_=ident[:], compare_op=ALU.not_equal, fill=1.0, base=0,
                            pattern=[[-1, P]], channel_multiplier=1)
            g.affine_select(out=upper[:, 0:P], in_=upper[:, 0:P], compare_op=ALU.is_ge, fill=0.0, base=0,
                            pattern=[[1, P]], channel_multiplier=-1)
            g.affine_select(out=causal_add[:], in_=causal_add[:], compare_op=ALU.is_ge, fill=MASKED, base=0,
                            pattern=[[-1, P]], channel_multiplier=1)
            g.affine_select(out=strict_add[:], in_=strict_add[:], compare_op=ALU.is_ge, fill=MASKED, base=-1,
                            pattern=[[-1, P]], channel_multiplier=1)
            g.affine_select(out=strict_mul[:], in_=strict_mul[:], compare_op=ALU.is_ge, fill=0.0, base=-1,
                            pattern=[[-1, P]], channel_multiplier=1).then_inc(consts_ready, 1)
            pool.wait_ge(norm_loaded, 32)
            for t in range(TT):
                ins = g.tensor_tensor(x_tok[:, t], x_tok[:, t], norm_rows[:, 0], ALU.mult)
            ins.then_inc(pool_done, 1)
            pool.wait_ge(pool_done, 2)
            for t in range(TT):
                ins = g.tensor_tensor(x_tok[:, t], x_tok[:, t], norm_rows[:, 1], ALU.add)
            ins.then_inc(residual_ready, 1)
            pool.wait_ge(norm_loaded, 64)
            for b in range(2):
                pool.wait_ge(aux_ready[b], mark["x1_transposed"][b])
            for t in range(TT):
                ins = g.tensor_tensor(x_tok[:, t], x_tok[:, t], norm_rows[:, 0], ALU.mult)
            ins.then_inc(pool_done, 1)
            pool.wait_ge(pool_done, 3)
            for t in range(TT):
                ins = g.tensor_tensor(x_tok[:, t], x_tok[:, t], norm_rows[:, 1], ALU.add)
            ins.then_inc(pool_done, 1)
            pool.wait_ge(pool_done, 4)
            g.tensor_scalar(x_tok[:], x_tok[:], ALPHA, None, ALU.mult).then_inc(residual_ready, 1)
            for t in range(TT):
                for m in range(CB):
                    cols = slice(m * NC, (m + 1) * NC)
                    pool.wait_ge(scaled_ready, t * CB + m + 1)
                    g.tensor_tensor(x_tok[:, t, cols], x_tok[:, t, cols], norm_rows[:, 1, cols],
                                    ALU.add).then_inc(y_ready, 1)

        @block.sync
        def _(sp):
            slab = Count(lo_ready)
            biases = Count(gate_in_ready)

            def load_slab(view):
                slot = slab.n % RING
                if slab.n >= RING:
                    sp.wait_ge(lo_ready, slab.value(RING - 1))
                sp.dma_start(w_raw[:, slot], view.rearrange("(k p) n -> p k n", p=P)).then_inc(slab_loaded[slot], 16)
                slab.next()

            def load_group(w, col, slabs=SLABS):
                for s in range(slabs):
                    load_slab(w[s * SLAB_K * P:(s + 1) * SLAB_K * P, bass.ds(col, NC)])

            def load_norm(gain, shift):
                sp.dma_start(norm_rows[:, 0], gain.partition_broadcast(P)).then_inc(norm_loaded, 16)
                sp.dma_start(norm_rows[:, 1], shift.partition_broadcast(P)).then_inc(norm_loaded, 16)

            for t in range(TT):
                sp.dma_start(x_tok[:, t, :], x[0, t * P:(t + 1) * P, :]).then_inc(x_loaded[t], 16)
            for j in range(2):
                load_group(w_in[0], LRU + j * NC)
            with loop(sp, 3, {slab: SLABS}) as j:
                load_group(w_in[0], FOX + j * NC)
            with loop(sp, 6, {slab: SLABS}) as j:
                load_group(w_in[0], STICK + j * NC)
            rel = rel_bias[0]
            sp.wait_ge(rel_mask_ready, 1)
            for half, first in ((0, CHUNK), (1, 0)):
                src = bass.AP(rel.tensor, rel.offset, [[1, CHUNK], [REL, HEADS], [1, SEQ - first]])
                sp.dma_start(band_bias[half * CHUNK:(half + 1) * CHUNK, :, first:], src).then_inc(rel_loaded, 16)

            def load_merge_row(col, first):
                for g in range(4):
                    if not first or g >= 2:
                        sp.wait_ge(gate_in_ready, biases.value(1))
                    sp.dma_start(b_gate_rows[:, g % 2], b_gate[0][g, bass.ds(col, NC)].partition_broadcast(P)
                                 ).then_inc(gate_bias_loaded[g % 2], 16)
                    biases.next()
                    load_group(w_gate[0][g], col)
                    load_group(w_branch[0][g], col, MIX_SLABS)

            load_merge_row(0, True)
            sp.wait_ge(aux_taken[1], mark["attention_done"])
            load_norm(ln_in_g, ln_in_b)
            with loop(sp, CB - 1, {slab: ROW_STEPS, biases: 4}) as n:
                load_merge_row(n * NC + NC, False)
            sp.wait_ge(residual_ready, 1)
            load_norm(ln1_g[0], ln1_b[0])
            with loop(sp, CB, {slab: SLABS}) as m:
                load_group(w_out[0], m * NC)
            with loop(sp, QUARTERS, {slab: QUARTER_STEPS}) as q:
                with loop(sp, CB, {slab: SLABS}) as i:
                    load_group(w_ff1[0], q * D + i * NC)
                with loop(sp, CB, {slab: SLABS}) as m:
                    for s in range(SLABS):
                        load_slab(w_ff2[0][bass.ds(q * D + s * SLAB_K * P, SLAB_K * P), bass.ds(m * NC, NC)])
            sp.wait_ge(residual_ready, 2)
            load_norm(ln2_g[0], ln2_b[0])
            for t in range(TT):
                for m in range(CB):
                    cols = slice(m * NC, (m + 1) * NC)
                    sp.wait_ge(y_ready, t * CB + m + 1)
                    sp.dma_start(out[0, t * P:(t + 1) * P, cols], x_tok[:, t, cols]).then_inc(out_stored, 16)
            sp.wait_ge(out_stored, 16 * TT * CB)


INPUTS = ["x", "ln_in_g", "ln_in_b", "w_in", "b_forget", "conv_w", "conv_b", "w_r", "b_r", "w_i", "b_i", "lru_lambda",
          "rel_bias", "w_branch", "w_gate", "b_gate", "w_out", "ln1_g", "ln1_b", "w_ff1", "w_ff2", "ln2_g", "ln2_b"]


def kernel(**inputs):
    import numpy as np
    import concourse.bacc as bacc
    from concourse.bass_utils import run_bass_kernel_spmd

    nc = bacc.Bacc("TRN2", target_bir_lowering=False, num_devices=1)
    arrays, args = {}, []
    for name in INPUTS:
        a = np.ascontiguousarray(inputs[name])
        arrays[f"in_{name}"] = a
        args.append(nc.dram_tensor(f"in_{name}", a.shape, mybir.dt.from_np(a.dtype), kind="ExternalInput").ap())
    args.append(nc.dram_tensor("out_x", (1, SEQ, D), F32, kind="ExternalOutput").ap())
    build(nc, *args)
    return run_bass_kernel_spmd(nc, [arrays], core_ids=[0]).results[0]["out_x"]
```

```python
from contextlib import ExitStack, contextmanager

import concourse.bass as bass
from concourse import mybir

F32 = mybir.dt.float32
F32R = mybir.dt.float32r
ALU = mybir.AluOpType
ACT = mybir.ActivationFunctionType
AX = mybir.AxisListType

P = 128
SEQ = 256
TT = SEQ // P
D = 2048
KT = D // P
NC = 512
CB = D // NC
HEADS = 4
CHUNK = 64
REL = 256 + CHUNK
CONV = 4
FF = 4 * D
SLAB_K = 2
SLABS = KT // SLAB_K
MIX_SLABS = NC // P // SLAB_K
RING = 4
LEAD = RING
IN_GROUPS = 11
QUARTERS = FF // D
GATE_STEPS = SLABS + MIX_SLABS
ROW_STEPS = 4 * GATE_STEPS
QUARTER_STEPS = 2 * CB * SLABS
ALPHA = 2.0 ** 0.25
SCALE = P ** -0.5
EPS = 1e-5
MASKED = -1e30
GELU_C = (2.0 / 3.141592653589793) ** 0.5
FOX, FORGET, LRU, STICK = 0, 3 * NC, 3 * NC + HEADS, 5 * NC + HEADS
LN_IN_G, LN_IN_B, LN1_G, LN1_B, CONV_W, CONV_B, B_R, B_I, LAM = 0, 16, 32, 48, 64, 80, 84, 88, 92
PARAMS = 96


class Count:

    def __init__(self, sem, start=0):
        self.sem, self.n, self.loops = sem, start, []

    def value(self, back=0):
        v = self.n - back
        for turn, per, _ in self.loops:
            v = turn * per + v
        return v

    def scaled(self, num, den):
        v = self.n // den * num
        for turn, per, _ in self.loops:
            assert per % den == 0
            v = turn * (per // den * num) + v
        return v

    def next(self, k=1):
        self.n += k
        return self.value()


@contextmanager
def loop(eng, trips, per):
    with eng.Fori(0, trips) as turn:
        for c, k in per.items():
            c.loops.append((turn, k, c.n))
        yield turn
        for c, k in per.items():
            _, _, start = c.loops.pop()
            assert c.n - start == k, (c.sem, c.n - start, k)
            c.n = start + k * trips


def build(nc, x, ln_in_g, ln_in_b, w_in, b_forget, conv_w, conv_b, w_r, b_r, w_i, b_i, lru_lambda,
          rel_bias, w_branch, w_gate, b_gate, w_out, ln1_g, ln1_b, w_ff1, w_ff2, ln2_g, ln2_b, out):
    with ExitStack() as ctx:
        top = [(nc.sbuf_base + 63) // 64 * 64]
        def place(name, shape, dtype=F32, at=None):
            size = 4
            for n in shape[1:]:
                size *= n
            if at is None:
                at = top[0]
                top[0] += (size + 63) // 64 * 64
            return nc.alloc_sbuf_tensor_at(name, shape, dtype, offset=at), at

        x_tok, _ = place("x_tok", [P, TT, D])
        xT_hi, _ = place("xT_hi", [P, KT, SEQ], F32R)
        xT_lo, _ = place("xT_lo", [P, KT, SEQ], F32R)
        zT_hi, z_at = place("zT_hi", [P, KT, SEQ], F32R)
        zT_lo, _ = place("zT_lo", [P, KT, SEQ], F32R)
        oT_hi, o_at = place("oT_hi", [P, 4, HEADS, SEQ], F32R)
        oT_lo, _ = place("oT_lo", [P, 4, HEADS, SEQ], F32R)
        w_raw, _ = place("w_raw", [P, RING, SLAB_K, NC])
        w_hi, _ = place("w_hi", [P, RING, SLAB_K, NC], F32R)
        w_lo, _ = place("w_lo", [P, RING, SLAB_K, NC], F32R)
        stage, _ = place("stage", [P, TT, NC])
        gate, _ = place("gate", [P, TT, NC])
        b_gate_rows, _ = place("b_gate_rows", [P, 2, NC])
        qT, att_at = place("qT", [P, HEADS, SEQ])
        kT, _ = place("kT", [P, HEADS, SEQ])
        v_tok, v_at = place("v_tok", [P, TT, NC])
        logits, logits_at = place("logits", [P, 2, 3 * P])
        stick_l, _ = place("stick_l", [P, 3 * P])
        stick_b, _ = place("stick_b", [P, 3 * P])
        stick_c, _ = place("stick_c", [P, 3 * P])
        probsT, probsT_at = place("probsT", [P, 3 * P])
        fox_bias, bias_at = place("fox_bias", [P, HEADS, 3 * P])
        band_bias, _ = place("band_bias", [P, HEADS, SEQ], at=bias_at)
        lru = [place(f"lru_{c}", [P, HEADS, SEQ], at=z_at + 4096 * i)[0] for i, c in enumerate("abcdef")]
        w_ri, _ = place("w_ri", [P, 2, HEADS, P], at=v_at)
        sig, _ = place("sig", [P, 6, SEQ + HEADS], at=logits_at)
        param_rows, _ = place("param_rows", [P, P], at=probsT_at)
        wf_hi, _ = place("wf_hi", [P, KT, P], F32R, at=o_at)
        wf_lo, _ = place("wf_lo", [P, KT, P], F32R, at=o_at + 4 * KT * P)
        norm_rows, _ = place("norm_rows", [P, 2, D], at=att_at)
        ident, _ = place("ident", [P, P])
        ones, _ = place("ones", [P, SEQ])
        causal_add, _ = place("causal_add", [P, P])
        strict_add, _ = place("strict_add", [P, P])
        strict_mul, _ = place("strict_mul", [P, P])
        params, _ = place("params", [P, PARAMS])
        wf_raw, _ = place("wf_raw", [P, KT, HEADS])
        bn, _ = place("bn", [P, TT, CB, 6])
        mean_var, _ = place("mean_var", [P, TT, 2])
        rstd, _ = place("rstd", [P, TT])
        peak, _ = place("peak", [P, 2])
        neg_peak, _ = place("neg_peak", [P, 2])
        total, _ = place("total", [P, 2])
        inv_total, _ = place("inv_total", [P, 2])
        b_forget_col, _ = place("b_forget_col", [P, 1])
        carry, _ = place("carry", [P, 1])
        cum_q, _ = place("cum_q", [P, TT, HEADS])
        lru_cols, _ = place("lru_cols", [P, 4, HEADS])
        assert top[0] <= nc.sbuf_usable_end, (top[0], nc.sbuf_usable_end)

        def psum(name):
            return ctx.enter_context(nc.psum_tensor(name, [P, NC], F32))
        acc = [[psum(f"acc{i}{t}") for t in range(TT)] for i in range(3)]
        aux = [psum("aux0"), psum("aux1")]

        def sem(name):
            return ctx.enter_context(nc.semaphore(name))
        x_loaded = [sem("x_loaded0"), sem("x_loaded1")]
        params_loaded = sem("params_loaded")
        small_loaded = sem("small_loaded")
        slab_loaded = [sem(f"slab_loaded{i}") for i in range(RING)]
        rel_loaded = sem("rel_loaded")
        gate_bias_loaded = [sem("gate_bias_loaded0"), sem("gate_bias_loaded1")]
        norm_loaded = sem("norm_loaded")
        out_stored = sem("out_stored")
        consts_ready = sem("consts_ready")
        hi_ready = sem("hi_ready")
        lo_ready = sem("lo_ready")
        slab_used = sem("slab_used")
        acc_taken = sem("acc_taken")
        aux_ready = [sem("aux_ready0"), sem("aux_ready1")]
        aux_taken = [sem("aux_taken0"), sem("aux_taken1")]
        var_ready = sem("var_ready")
        std_ready = sem("std_ready")
        xn_ready = sem("xn_ready")
        evac_hi = sem("evac_hi")
        wf_hi_ready = sem("wf_hi_ready")
        wf_ready = sem("wf_ready")
        u_taken = sem("u_taken")
        sig_in = sem("sig_in")
        sig_exp = sem("sig_exp")
        cum_ready = sem("cum_ready")
        row0_ready = sem("row0_ready")
        normed_ready = sem("normed_ready")
        conv_ready = sem("conv_ready")
        lru_cols_ready = sem("lru_cols_ready")
        gated_x_ready = sem("gated_x_ready")
        decay_exp_ready = sem("decay_exp_ready")
        decay_tanh_ready = sem("decay_tanh_ready")
        rest_ready = sem("rest_ready")
        root_ready = sem("root_ready")
        gelu_in_ready = sem("gelu_in_ready")
        gelu_tanh_ready = sem("gelu_tanh_ready")
        lru_out_ready = sem("lru_out_ready")
        branch_done = sem("branch_done")
        peak_ready = sem("peak_ready")
        exp_ready = sem("exp_ready")
        probs_ready = sem("probs_ready")
        stick_log_ready = sem("stick_log_ready")
        stick_logits_ready = sem("stick_logits_ready")
        rel_mask_ready = sem("rel_mask_ready")
        gate_in_ready = sem("gate_in_ready")
        gate_ready = sem("gate_ready")
        mix_taken = sem("mix_taken")
        merged_ready = sem("merged_ready")
        relu_ready = sem("relu_ready")
        residual_ready = sem("residual_ready")
        act_done = sem("act_done")
        dve_done = sem("dve_done")
        pool_done = sem("pool_done")
        y_ready = sem("y_ready")
        gained_ready = sem("gained_ready")
        inv_ready = sem("inv_ready")
        scaled_ready = sem("scaled_ready")
        y1_ready = sem("y1_ready")

        def repeated(tile):
            return tile.rearrange("p k (r h) -> p k r h", h=HEADS)
        wf_wide = wf_raw[:].unsqueeze(2).to_broadcast([P, KT, P // HEADS, HEADS])

        block = ctx.enter_context(nc.Block())
        mark = {}

        @block.tensor
        def _(pe):
            slab = Count(slab_used)
            job = [Count(aux_taken[0]), Count(aux_taken[1])]
            projected = Count(u_taken)
            gated = Count(gate_in_ready)
            groups = Count(acc_taken)

            def free(b):
                if job[b].n:
                    pe.wait_ge(aux_taken[b], job[b].value())
                job[b].next()

            def start_projection():
                if projected.n >= 2:
                    pe.wait_ge(u_taken, projected.value(1))
                projected.next()

            def start_gate():
                if gated.n >= 2:
                    pe.wait_ge(gate_in_ready, gated.value(1))
                else:
                    pe.wait_ge(u_taken, IN_GROUPS - 1)
                gated.next()

            def start_group():
                if groups.n >= 2:
                    pe.wait_ge(acc_taken, groups.value(1))
                else:
                    pe.wait_ge(gate_in_ready, gated.value(1 - groups.n))
                groups.next()

            def products(pair, hi, lo, slabs, first, last):
                for s in slabs:
                    slot = slab.n % RING
                    slab.next()
                    pe.wait_ge(lo_ready, slab.value())
                    for kk in range(SLAB_K):
                        k = s * SLAB_K + kk
                        for t in range(TT):
                            toks = slice(t * P, (t + 1) * P)
                            begin = s == first and kk == 0
                            end = s == last and kk == SLAB_K - 1
                            nc.tensor.matmul(acc[pair][t][:], hi[:, k, toks], w_hi[:, slot, kk], start=begin, stop=False)
                            nc.tensor.matmul(acc[pair][t][:], hi[:, k, toks], w_lo[:, slot, kk], start=False, stop=False)
                            mm = nc.tensor.matmul(acc[pair][t][:], lo[:, k, toks], w_hi[:, slot, kk], start=False, stop=end)
                    mm.then_inc(slab_used, 1)

            def rows_apart(pair, hi, lo, slabs, last):
                slots = []
                for s in slabs:
                    slots.append(slab.n % RING)
                    slab.next()
                for t in range(TT):
                    for n, s in enumerate(slabs):
                        if t == 0:
                            pe.wait_ge(lo_ready, slab.value(len(slabs) - 1 - n))
                        for kk in range(SLAB_K):
                            k = s * SLAB_K + kk
                            toks = slice(t * P, (t + 1) * P)
                            end = s == last and kk == SLAB_K - 1
                            w, wl = w_hi[:, slots[n], kk], w_lo[:, slots[n], kk]
                            nc.tensor.matmul(acc[pair][t][:], hi[:, k, toks], w, start=False, stop=False)
                            nc.tensor.matmul(acc[pair][t][:], hi[:, k, toks], wl, start=False, stop=False)
                            mm = nc.tensor.matmul(acc[pair][t][:], lo[:, k, toks], w, start=False, stop=end)
                        if t == 1:
                            mm.then_inc(slab_used, 1)
                        elif s == last:
                            mm.then_inc(row0_ready, 1)

            def slabs_of(pair, hi, lo, slabs, total=SLABS):
                products(pair, hi, lo, slabs, 0, total - 1)

            def transpose_tokens(pair):
                b = pair % 2
                free(b)
                for kk in range(2):
                    k = 2 * pair + kk
                    for t in range(TT):
                        mm = nc.tensor.transpose(aux[b][:, kk * SEQ + t * P:kk * SEQ + (t + 1) * P],
                                                 x_tok[:, t, k * P:(k + 1) * P], ident[:])
                mm.then_inc(aux_ready[b], 1)

            def transpose_stage():
                for b in range(2):
                    free(b)
                    for kk in range(2):
                        k = 2 * b + kk
                        for t in range(TT):
                            mm = nc.tensor.transpose(aux[b][:, kk * SEQ + t * P:kk * SEQ + (t + 1) * P],
                                                     stage[:, t, k * P:(k + 1) * P], ident[:])
                    mm.then_inc(aux_ready[b], 1)

            def transpose_projected():
                pe.wait_ge(u_taken, projected.value(1))
                transpose_stage()

            def transpose_hidden(back):
                pe.wait_ge(acc_taken, groups.value(back))
                transpose_stage()

            pe.wait_ge(consts_ready, 1)
            pe.wait_ge(params_loaded, 16 * 9)
            free(0)
            nc.tensor.transpose(aux[0][:, 0:PARAMS], param_rows[0:PARAMS, :],
                                ident[0:PARAMS, 0:PARAMS]).then_inc(aux_ready[0], 1)
            normed = Count(normed_ready)

            def first_group(start, xn):
                pe.wait_ge(xn_ready, xn + 3)
                transpose_tokens(0)
                transpose_tokens(1)
                pe.wait_ge(xn_ready, xn + 4)
                start()
                for s in range(SLABS):
                    pe.wait_ge(normed_ready, normed.next())
                    slabs_of(0, xT_hi, xT_lo, [s])
                    if s + 2 < SLABS:
                        transpose_tokens(s + 2)

            first_group(start_projection, 0)

            start_projection()
            slabs_of(1, xT_hi, xT_lo, [0])
            free(0)
            pe.wait_ge(wf_ready, 1)
            for k in range(KT):
                nc.tensor.matmul(aux[0][:, 0:SEQ], wf_hi[:, k], xT_hi[:, k], start=k == 0, stop=False)
                nc.tensor.matmul(aux[0][:, 0:SEQ], wf_hi[:, k], xT_lo[:, k], start=False, stop=False)
                mm = nc.tensor.matmul(aux[0][:, 0:SEQ], wf_lo[:, k], xT_hi[:, k], start=False, stop=k == KT - 1)
            mm.then_inc(aux_ready[0], 1)
            slabs_of(1, xT_hi, xT_lo, [1, 2])
            transpose_projected()
            slabs_of(1, xT_hi, xT_lo, [3, 4, 5, 6, 7])

            def recurrent_gate(which):
                for b in range(2):
                    free(b)
                    for hh in range(2):
                        n = 2 * b + hh
                        mm = nc.tensor.matmul(aux[b][:, hh * SEQ:(hh + 1) * SEQ], w_ri[:, which, n],
                                              lru[2][:, n, :], start=True, stop=True)
                    mm.then_inc(aux_ready[b], 1)

            start_projection()
            slabs_of(0, xT_hi, xT_lo, [0, 1, 2])
            transpose_projected()
            slabs_of(0, xT_hi, xT_lo, [3, 4])
            pe.wait_ge(conv_ready, 1)
            pe.wait_ge(small_loaded, 16 * 4)
            recurrent_gate(0)
            slabs_of(0, xT_hi, xT_lo, [5, 6])
            recurrent_gate(1)
            slabs_of(0, xT_hi, xT_lo, [7])
            for pair in (1, 2):
                start_projection()
                slabs_of(pair, xT_hi, xT_lo, [0])
                if pair == 1:
                    pe.wait_ge(cum_ready, 1)
                    free(0)
                    for t in range(TT):
                        mm = nc.tensor.transpose(aux[0][:, t * P:(t + 1) * P], sig[:, 3, t * P:(t + 1) * P], ident[:])
                    mm.then_inc(aux_ready[0], 1)
                slabs_of(pair, xT_hi, xT_lo, [1])
                if pair == 1:
                    for b in range(2):
                        free(b)
                        for hh in range(2):
                            h = 2 * b + hh
                            mm = nc.tensor.matmul(aux[b][:, hh * SEQ:(hh + 1) * SEQ],
                                                  ident[:, h:h + 1].to_broadcast([P, P]), sig[:, 3, 0:SEQ],
                                                  start=True, stop=True)
                        mm.then_inc(aux_ready[b], 1)
                slabs_of(pair, xT_hi, xT_lo, [2])
                transpose_projected()
                slabs_of(pair, xT_hi, xT_lo, [3, 4, 5, 6, 7])

            ready = Count(probs_ready)
            values_back = [1]

            def scores(h):
                free(0)
                nc.tensor.matmul(aux[0][:, 0:P], qT[:, h, 0:P], kT[:, h, 0:P], start=True, stop=True)
                nc.tensor.matmul(aux[0][:, P:3 * P], qT[:, h, P:SEQ], kT[:, h, :],
                                 start=True, stop=True).then_inc(aux_ready[0], 1)

            def transpose_probs(h):
                pe.wait_ge(probs_ready, ready.next())
                free(1)
                p = logits[:, h % 2]
                for i in range(3):
                    mm = nc.tensor.transpose(aux[1][:, i * P:(i + 1) * P], p[:, i * P:(i + 1) * P], ident[:])
                mm.then_inc(aux_ready[1], 1)

            def mix(h):
                free(1)
                vh = slice(h * P, (h + 1) * P)
                nc.tensor.matmul(aux[1][:, 0:P], v_tok[:, 0, vh], probsT[:, 0:P], start=True, stop=True)
                nc.tensor.matmul(aux[1][:, P:SEQ], v_tok[:, 0, vh], probsT[:, P:SEQ], start=True, stop=False)
                nc.tensor.matmul(aux[1][:, P:SEQ], v_tok[:, 1, vh], probsT[:, SEQ:3 * P],
                                 start=False, stop=True).then_inc(aux_ready[1], 1)

            def attention_after(step):
                h = step // 3
                if step == 0:
                    pe.wait_ge(aux_taken[1], job[1].value())
                if step == 4:
                    pe.wait_ge(u_taken, projected.value(values_back[0]))
                if step % 3 == 0 and 1 <= h <= HEADS:
                    transpose_probs(h - 1)
                if step % 3 == 1 and 1 <= h <= HEADS:
                    mix(h - 1)
                if step % 3 == 0 and h < HEADS:
                    scores(h)

            per = {slab: 3 * SLABS, projected: 3, ready: HEADS, job[0]: HEADS + 2, job[1]: 2 * HEADS + 2}
            with loop(pe, 2, per):
                for pair in range(3):
                    start_projection()
                    for s in range(SLABS):
                        slabs_of(pair, xT_hi, xT_lo, [s])
                        step = pair * SLABS + s
                        attention_after(step)
                        if step in (14, 18):
                            transpose_projected()

            merged = Count(merged_ready)
            mixed = Count(mix_taken)

            def merge_row(first):
                for g in range(4):
                    start_gate()
                    for s in range(SLABS):
                        slabs_of(g % 2, xT_hi, xT_lo, [s])
                        step = g * GATE_STEPS + s
                        if first:
                            attention_after(step)
                        elif step == 2:
                            pe.wait_ge(merged_ready, merged.next())
                            transpose_stage()
                    if first and g == 0:
                        pe.wait_ge(u_taken, IN_GROUPS)
                    else:
                        pe.wait_ge(mix_taken, mixed.value())
                    if first:
                        if g == 1:
                            pe.wait_ge(branch_done, 1)
                        if g == 3:
                            pe.wait_ge(aux_taken[1], job[1].value())
                    mixed.next()
                    for s in range(MIX_SLABS):
                        products(2, oT_hi[:, g], oT_lo[:, g], [s], 0, MIX_SLABS - 1)
                        if first:
                            attention_after(g * GATE_STEPS + SLABS + s)

            values_back[0] = 0
            merge_row(True)
            mark["attention_done"] = job[1].n
            with loop(pe, CB - 1, {slab: ROW_STEPS, gated: 4, merged: 1, mixed: 4, job[0]: 1, job[1]: 1}):
                merge_row(False)

            for m in range(CB):
                start_group()
                if m == 0:
                    slabs_of(0, zT_hi, zT_lo, [0, 1, 2])
                    pe.wait_ge(merged_ready, merged.next())
                    transpose_stage()
                    slabs_of(0, zT_hi, zT_lo, [3, 4, 5])
                    for b in range(2):
                        pe.wait_ge(aux_taken[b], job[b].value())
                    slabs_of(0, zT_hi, zT_lo, [6, 7])
                elif m < CB - 1:
                    slabs_of(m % 2, zT_hi, zT_lo, range(SLABS))
                else:
                    slabs_of(m % 2, zT_hi, zT_lo, range(SLABS - LEAD))
                    rows_apart(m % 2, zT_hi, zT_lo, range(SLABS - LEAD, SLABS), SLABS - 1)

            first_group(start_group, 4)
            mark["x1_transposed"] = [job[0].n, job[1].n]
            with loop(pe, QUARTERS, {slab: QUARTER_STEPS, groups: 2 * CB, job[0]: CB, job[1]: CB}) as q:
                for i in range(1, CB):
                    start_group()
                    slabs_of(i % 2, xT_hi, xT_lo, [0, 1, 2])
                    transpose_hidden(1)
                    slabs_of(i % 2, xT_hi, xT_lo, [3, 4, 5, 6, 7])
                for b in range(2):
                    pe.wait_ge(aux_taken[b], job[b].value())
                for i in range(CB):
                    start_group()
                    if i == 0:
                        slabs_of(0, zT_hi, zT_lo, [0, 1, 2])
                        transpose_hidden(1)
                        slabs_of(0, zT_hi, zT_lo, [3, 4, 5])
                        for b in range(2):
                            pe.wait_ge(aux_taken[b], job[b].value())
                        slabs_of(0, zT_hi, zT_lo, [6, 7])
                    elif i < CB - 1:
                        slabs_of(i % 2, zT_hi, zT_lo, range(SLABS))
                    else:
                        slabs_of(i % 2, zT_hi, zT_lo, range(SLABS - LEAD))
                        rows_apart(i % 2, zT_hi, zT_lo, range(SLABS - LEAD, SLABS), SLABS - 1)
                with pe.If(QUARTERS - 1 - q):
                    start_group()
                    slabs_of(0, xT_hi, xT_lo, range(SLABS))

        @block.scalar
        def _(act):
            slab = Count(hi_ready)
            job = [Count(aux_ready[0]), Count(aux_ready[1])]
            done = Count(act_done)
            std = Count(std_ready)
            hi_out = Count(evac_hi)

            def split(n):
                for _ in range(n):
                    slot = slab.n % RING
                    act.wait_ge(slab_loaded[slot], slab.scaled(16, RING) + 16)
                    if slab.n >= RING:
                        act.wait_ge(slab_used, slab.value(RING - 1))
                    nc.scalar.copy(w_hi[:, slot], w_raw[:, slot]).then_inc(hi_ready, 1)
                    slab.next()

            def settle():
                act.wait_ge(act_done, done.value())

            def did(ins):
                ins.then_inc(act_done, 1)
                done.next()

            def wait_job(b):
                act.wait_ge(aux_ready[b], job[b].next())

            def skip_job(b):
                job[b].next()

            def root(t):
                act.wait_ge(var_ready, std.next())
                nc.scalar.activation(rstd[:, t:t + 1], mean_var[:, t, 1:2], ACT.Sqrt).then_inc(std_ready, 1)

            normed = Count(normed_ready)

            def normed_pair(pair, gain, shift):
                b = pair % 2
                wait_job(b)
                if normed.n >= 2:
                    act.wait_ge(normed_ready, normed.value(1))
                normed.next()
                for kk in range(2):
                    k = 2 * pair + kk
                    ins = nc.scalar.activation(gate[:, b, kk * SEQ:(kk + 1) * SEQ], aux[b][:, kk * SEQ:(kk + 1) * SEQ],
                                               ACT.Identity, scale=params[:, gain + k:gain + k + 1],
                                               bias=params[:, shift + k:shift + k + 1])
                ins.then_inc(aux_taken[b], 1)

            rows = [(ln_in_g, LN_IN_G), (ln_in_b, LN_IN_B), (ln1_g[0], LN1_G), (ln1_b[0], LN1_B),
                    (conv_w[0].rearrange("j c -> (j c)"), CONV_W), (conv_b[0], CONV_B), (b_r[0], B_R),
                    (b_i[0], B_I), (lru_lambda[0], LAM)]
            for vec, at in rows:
                n = vec.shape[0] // P
                act.dma_start(param_rows[at:at + n, :], vec.rearrange("(k p) -> k p", p=P)).then_inc(params_loaded, 16)
            act.dma_start(wf_raw[:], w_in[0][:, FORGET:FORGET + HEADS].rearrange("(k p) n -> p k n", p=P)).then_inc(small_loaded, 16)
            act.dma_start(w_ri[:, 0], w_r[0].rearrange("n c d -> c n d")).then_inc(small_loaded, 16)
            act.dma_start(w_ri[:, 1], w_i[0].rearrange("n c d -> c n d")).then_inc(small_loaded, 16)
            act.dma_start(b_forget_col[:], bass.AP(b_forget.tensor, b_forget.offset, [[0, P // HEADS], [1, HEADS], [1, 1]])
                          ).then_inc(small_loaded, 16)
            for t in range(TT):
                root(t)
            split(1)
            skip_job(0)
            act.wait_ge(aux_taken[0], 1)
            normed_pair(0, LN_IN_G, LN_IN_B)
            split(1)
            normed_pair(1, LN_IN_G, LN_IN_B)
            split(2)
            for s in range(SLABS):
                split(1)
                if s + 2 < SLABS:
                    normed_pair(s + 2, LN_IN_G, LN_IN_B)

            def to_rows(rows, pair):
                act.wait_ge(slab_used, slab.value(LEAD))
                nc.scalar.copy(rows[:, 0, :], acc[pair][0][:])
                nc.scalar.copy(rows[:, 1, :], acc[pair][1][:]).then_inc(u_taken, 1)

            def from_stage(to):
                for b in range(2):
                    wait_job(b)
                    nc.scalar.copy(to[:, 2 * b:2 * b + 2, :],
                                   aux[b][:].rearrange("p (k t) -> p k t", k=2)).then_inc(aux_taken[b], 1)

            def recurrent_gate(to, which):
                for b in range(2):
                    wait_job(b)
                    for hh in range(2):
                        n = 2 * b + hh
                        ins = nc.scalar.activation(to[:, n, :], aux[b][:, hh * SEQ:(hh + 1) * SEQ], ACT.Tanh,
                                                   scale=0.5, bias=lru_cols[:, which, n:n + 1])
                    ins.then_inc(aux_taken[b], 1)

            def decay(to, func, which, signal):
                for n in range(HEADS):
                    c = lru_cols[:, which, n:n + 1]
                    ins = nc.scalar.activation(to[:, n, :], lru[3][:, n, :], func, scale=c, bias=c)
                ins.then_inc(signal, 1)

            a, b_, c_, d_, e_, f_ = lru
            to_rows(stage, 0)
            act.wait_ge(small_loaded, 16 * 4)
            nc.scalar.copy(repeated(wf_hi[:]), wf_wide).then_inc(wf_hi_ready, 1)
            split(1)
            skip_job(0)
            act.wait_ge(sig_in, 1)
            nc.scalar.activation(sig[:, 2, :], sig[:, 1, :], ACT.Exp).then_inc(sig_exp, 1)
            split(2)
            from_stage(a)
            split(5)
            to_rows(stage, 1)
            split(3)
            from_stage(b_)
            split(2)
            act.wait_ge(lru_cols_ready, 1)
            recurrent_gate(d_, 0)
            split(2)
            recurrent_gate(e_, 1)
            act.wait_ge(aux_taken[1], job[1].value())
            skip_job(0)
            skip_job(0)
            skip_job(1)
            split(1)
            to_rows(stage, 0)
            split(1)
            decay(a, ACT.Exp, 2, decay_exp_ready)
            split(1)
            decay(f_, ACT.Tanh, 2, decay_tanh_ready)
            split(1)
            from_stage(qT)
            split(2)
            act.wait_ge(gated_x_ready, 1)
            decay(c_, ACT.Tanh, 3, decay_tanh_ready)
            split(3)
            to_rows(stage, 1)
            act.wait_ge(rest_ready, 1)
            nc.scalar.activation(f_[:], a[:], ACT.Sqrt, scale=-1.0).then_inc(root_ready, 1)
            split(3)
            from_stage(kT)
            split(1)
            act.wait_ge(gelu_in_ready, 1)
            nc.scalar.activation(f_[:], c_[:], ACT.Tanh, scale=GELU_C).then_inc(gelu_tanh_ready, 1)
            split(2)
            act.wait_ge(lru_out_ready, 1)
            nc.scalar.copy(oT_hi[:, 1], c_[:]).then_inc(evac_hi, 1)
            hi_out.next()
            split(2)
            to_rows(v_tok, 2)

            peaks = Count(peak_ready)
            stick = Count(stick_logits_ready)

            def probs_out(h):
                wait_job(1)
                nc.scalar.copy(probsT[:], aux[1][:, 0:3 * P]).then_inc(aux_taken[1], 1)

            def mixed_out(branch, h):
                wait_job(1)
                nc.scalar.copy(oT_hi[:, branch, h, :], aux[1][:, 0:SEQ]).then_inc(evac_hi, 1)
                hi_out.next()

            def softmax_exp(h):
                act.wait_ge(peak_ready, peaks.next())
                p = logits[:, h % 2]
                nc.scalar.activation(p[:, 0:P], p[:, 0:P], ACT.Exp, bias=neg_peak[:, 0:1], accum_out=total[:, 0:1])
                nc.scalar.activation(p[:, P:3 * P], p[:, P:3 * P], ACT.Exp, bias=neg_peak[:, 1:2],
                                     accum_out=total[:, 1:2]).then_inc(exp_ready, 1)

            def stick_log(h):
                wait_job(0)
                did(nc.scalar.activation(stick_l[:], aux[0][:, 0:3 * P], ACT.Abs, scale=SCALE))
                settle()
                did(nc.scalar.activation(stick_l[:], stick_l[:], ACT.Exp, scale=-1.0))
                settle()
                nc.scalar.activation(stick_l[:], stick_l[:], ACT.Ln, bias=1.0).then_inc(stick_log_ready, 1)

            def stick_exp(h):
                act.wait_ge(stick_logits_ready, stick.next())
                p = logits[:, h % 2]
                nc.scalar.activation(p, p, ACT.Exp).then_inc(probs_ready, 1)

            def attention_step(branch, step, stick_breaking):
                h = step // 3
                if step % 3 == 0:
                    if 1 <= h <= HEADS:
                        probs_out(h - 1)
                    if h < HEADS:
                        if stick_breaking:
                            stick_log(h)
                        else:
                            skip_job(0)
                if step % 3 == 1:
                    if 1 <= h <= HEADS:
                        mixed_out(branch, h - 1)
                    if h < HEADS and not stick_breaking:
                        softmax_exp(h)
                if step % 3 == 2 and h < HEADS and stick_breaking:
                    stick_exp(h)

            for branch in (0, 2):
                for step in range(3 * SLABS):
                    split(1)
                    attention_step(branch, step, branch == 2)
                    if step == 7:
                        to_rows(stage, 0)
                    if step == 14:
                        from_stage(qT)
                    if step == 15:
                        to_rows(stage, 1)
                    if step == 18:
                        from_stage(kT)
                    if step == 23:
                        to_rows(v_tok, 2)

            gates = Count(gate_in_ready)

            def halves_out(hi_to, b, scale=1.0):
                nc.scalar.activation(hi_to, aux[b][:].rearrange("p (k t) -> p k t", k=2), ACT.Copy,
                                     scale=scale).then_inc(evac_hi, 1)
                hi_out.next()

            def merge_row(first, n=None):
                for step in range(ROW_STEPS):
                    g, s = divmod(step, GATE_STEPS)
                    if not first and step == 3:
                        for b in range(2):
                            wait_job(b)
                    split(1)
                    if first:
                        attention_step(3, step, False)
                    elif step == 3:
                        for b in range(2):
                            k = n * (NC // P) + 2 * b
                            halves_out(zT_hi[:, bass.ds(k, 2), :], b, 0.5)
                    if s == SLABS:
                        act.wait_ge(gate_in_ready, gates.next())
                        nc.scalar.activation(gate[:], gate[:], ACT.Tanh, scale=0.5).then_inc(gate_ready, 1)

            merge_row(True)
            with loop(act, CB - 1, {slab: ROW_STEPS, job[0]: 1, job[1]: 1, hi_out: 2, gates: 4}) as n:
                merge_row(False, n)

            split(3)
            for b in range(2):
                wait_job(b)
                halves_out(zT_hi[:, (CB - 1) * (NC // P) + 2 * b:(CB - 1) * (NC // P) + 2 * b + 2, :], b, 0.5)
            split(CB * SLABS - LEAD - 3)

            root(0)
            split(LEAD - 1)
            root(1)
            split(1)
            normed_pair(0, LN1_G, LN1_B)
            normed_pair(1, LN1_G, LN1_B)
            relus = Count(relu_ready)

            def relu(pair):
                act.wait_ge(slab_used, slab.value(LEAD))
                nc.scalar.activation(stage[:, 0], acc[pair][0][:], ACT.Relu)
                nc.scalar.activation(stage[:, 1], acc[pair][1][:], ACT.Relu).then_inc(relu_ready, 1)
                relus.next()

            for s in range(SLABS):
                split(1)
                if s + 2 < SLABS:
                    normed_pair(s + 2, LN1_G, LN1_B)
            relu(0)

            with loop(act, QUARTERS, {slab: QUARTER_STEPS, job[0]: CB, job[1]: CB, hi_out: 2 * CB, relus: CB}) as q:
                for step in range(SLABS, QUARTER_STEPS - LEAD):
                    split(1)
                    i, s = divmod(step, SLABS)
                    if s == 2 and i <= CB:
                        for b in range(2):
                            wait_job(b)
                            k = (i - 1) * (NC // P) + 2 * b
                            halves_out(zT_hi[:, k:k + 2, :], b)
                    if s == SLABS - 1 and i < CB:
                        relu(i % 2)
                with act.If(QUARTERS - 1 - q):
                    split(LEAD + SLABS)
                    relu(0)
            for t in range(TT):
                root(t)
            for m in range(CB):
                cols = slice(m * NC, (m + 1) * NC)
                act.wait_ge(gained_ready, m + 1)
                if m == 0:
                    act.wait_ge(inv_ready, 1)
                nc.scalar.activation(x_tok[:, 0, cols], x_tok[:, 0, cols], ACT.Copy, scale=rstd[:, 0:1]).then_inc(scaled_ready, 1)

        @block.vector
        def _(dve):
            slab = Count(lo_ready)
            job = [Count(aux_ready[0]), Count(aux_ready[1])]
            done = Count(dve_done)
            std = Count(std_ready)
            hi_in = Count(evac_hi)
            acc_done = Count(acc_taken)
            v = nc.vector

            def split(n):
                for _ in range(n):
                    slot = slab.n % RING
                    dve.wait_ge(hi_ready, slab.next())
                    v.tensor_sub(w_lo[:, slot], w_raw[:, slot], w_hi[:, slot]).then_inc(lo_ready, 1)

            def did(ins):
                ins.then_inc(dve_done, 1)
                done.next()

            def settle():
                dve.wait_ge(dve_done, done.value())

            def chain(ins):
                did(ins)
                settle()

            def wait_job(b):
                dve.wait_ge(aux_ready[b], job[b].next())

            def skip_job(b):
                job[b].next()

            def statistics(t, m):
                did(v.bn_stats(bn[:, t, m], x_tok[:, t, m * NC:(m + 1) * NC]))

            def spread(t):
                settle()
                chain(v.bn_aggr(mean_var[:, t], bn[:, t].rearrange("p m s -> p (m s)")))
                v.tensor_scalar(mean_var[:, t, 1:2], mean_var[:, t, 1:2], EPS, None, ALU.add).then_inc(var_ready, 1)

            def normalise(t):
                dve.wait_ge(std_ready, std.next())
                chain(v.reciprocal(rstd[:, t:t + 1], rstd[:, t:t + 1]))
                for cols in (slice(0, NC), slice(NC, D)):
                    v.tensor_scalar(x_tok[:, t, cols], x_tok[:, t, cols], mean_var[:, t, 0:1], rstd[:, t:t + 1],
                                    ALU.subtract, ALU.mult).then_inc(xn_ready, 1)

            normed = Count(normed_ready)

            def normed_pair(pair):
                b = pair % 2
                skip_job(b)
                dve.wait_ge(aux_taken[b], job[b].value())
                ks = slice(2 * pair, 2 * pair + 2)
                full = gate[:, b].rearrange("p (k t) -> p k t", k=2)
                chain(v.tensor_copy(xT_hi[:, ks], full))
                v.tensor_sub(xT_lo[:, ks], full, xT_hi[:, ks]).then_inc(normed_ready, 1)

            did(v.memset(carry[:], ALPHA))
            for t in range(TT):
                dve.wait_ge(x_loaded[t], 16)
                for m in range(CB):
                    statistics(t, m)
                spread(t)
            for t in range(TT):
                normalise(t)
            wait_job(0)
            v.tensor_copy(params[:], aux[0][:, 0:PARAMS]).then_inc(aux_taken[0], 1)
            split(1)
            normed_pair(0)
            split(1)
            normed_pair(1)
            split(2)
            for s in range(SLABS):
                if s + 2 < SLABS:
                    normed_pair(s + 2)
                split(1)

            a, b_, c_, d_, e_, f_ = lru
            arg, neg, ex, s1, s2, acc_ = [sig[:, i] for i in range(6)]
            dve.wait_ge(wf_hi_ready, 1)
            v.tensor_sub(repeated(wf_lo[:]), wf_wide, repeated(wf_hi[:])).then_inc(wf_ready, 1)
            wait_job(0)
            did(v.tensor_copy(arg[:, SEQ:], params[:, LAM:LAM + HEADS]))
            v.tensor_scalar(arg[:, 0:SEQ], aux[0][:, 0:SEQ], b_forget_col[:], None, ALU.add).then_inc(aux_taken[0], 1)
            dve.wait_ge(aux_taken[0], job[0].value())
            v.scalar_tensor_tensor(neg, arg, -1.0, arg, ALU.mult, ALU.min).then_inc(sig_in, 1)
            did(v.tensor_scalar(lru_cols[:, 0], params[:, B_R:B_R + HEADS], 0.5, None, ALU.mult))
            did(v.tensor_scalar(lru_cols[:, 1], params[:, B_I:B_I + HEADS], 0.5, None, ALU.mult))
            split(3)

            skip_job(0)
            skip_job(1)
            dve.wait_ge(aux_taken[0], job[0].value())
            dve.wait_ge(aux_taken[1], job[1].value())
            for n in range(HEADS):
                tap = [params[:, CONV_W + j * HEADS + n:CONV_W + j * HEADS + n + 1] for j in range(CONV)]
                chain(v.tensor_scalar(c_[:, n], a[:, n], tap[CONV - 1], params[:, CONV_B + n:CONV_B + n + 1],
                                      ALU.mult, ALU.add))
                for j in reversed(range(CONV - 1)):
                    lag = CONV - 1 - j
                    ins = v.scalar_tensor_tensor(c_[:, n, lag:], a[:, n, 0:SEQ - lag], tap[j], c_[:, n, lag:],
                                                 ALU.mult, ALU.add)
                    if j or n < HEADS - 1:
                        chain(ins)
                if n < HEADS - 1:
                    split(1)
            ins.then_inc(conv_ready, 1)
            split(1)

            dve.wait_ge(sig_exp, 1)
            chain(v.tensor_scalar(s1, ex, 2.0, None, ALU.add))
            chain(v.reciprocal(s1, s1))
            split(1)
            chain(v.tensor_tensor(s1, s1, ex, ALU.mult))
            chain(v.tensor_tensor(s2, s1, s1, ALU.mult))
            chain(v.tensor_scalar(acc_, s2, 1.0 / 15, None, ALU.mult))
            split(1)
            for odd in (13, 11, 9, 7, 5, 3):
                chain(v.scalar_tensor_tensor(acc_, acc_, 1.0 / odd, s2, ALU.add, ALU.mult))
                if odd == 9:
                    split(1)
            split(1)
            chain(v.scalar_tensor_tensor(acc_, acc_, 1.0, s1, ALU.add, ALU.mult))
            chain(v.tensor_scalar(neg, arg, 0.0, None, ALU.min))
            chain(v.scalar_tensor_tensor(acc_, acc_, -2.0, neg, ALU.mult, ALU.add))
            did(v.tensor_scalar(lru_cols[:, 2], acc_[:, SEQ:], 4.0, None, ALU.mult))
            v.tensor_scalar(lru_cols[:, 3], acc_[:, SEQ:], 2.0, None, ALU.mult).then_inc(lru_cols_ready, 1)
            split(1)
            v.tensor_tensor_scan(sig[:, 3, 0:SEQ], ones[:], acc_[:, 0:SEQ], 0.0, ALU.mult, ALU.add).then_inc(cum_ready, 1)

            for _ in range(2):
                skip_job(0)
                skip_job(1)
            split(3)
            skip_job(0)
            skip_job(1)
            for b in range(2):
                dve.wait_ge(aux_taken[b], job[b].value())
            v.scalar_tensor_tensor(e_[:], e_[:], 1.0, c_[:], ALU.add, ALU.mult).then_inc(gated_x_ready, 1)
            split(2)

            wait_job(0)
            v.tensor_copy(cum_q[:], aux[0][:, 0:SEQ].rearrange("p (t r) -> p t r", t=TT)[:, :, 0:HEADS]
                          ).then_inc(aux_taken[0], 1)
            split(1)
            dve.wait_ge(aux_taken[0], job[0].value())
            for b in range(2):
                wait_job(b)
                for hh in range(2):
                    h = 2 * b + hh
                    sums = aux[b][:, hh * SEQ:(hh + 1) * SEQ]
                    did(v.tensor_scalar(fox_bias[:, h, 0:P], sums[:, 0:P], -1.0, cum_q[:, 0, h:h + 1], ALU.mult, ALU.add))
                    ins = v.tensor_scalar(fox_bias[:, h, P:3 * P], sums, -1.0, cum_q[:, 1, h:h + 1], ALU.mult, ALU.add)
                    if hh == 0:
                        did(ins)
                ins.then_inc(aux_taken[b], 1)
                dve.wait_ge(aux_taken[b], job[b].value())
                split(1)
            settle()
            diagonal = fox_bias[:].rearrange("p h (c k) -> p h c k", k=P)[:, :, 0::2, :]
            chain(v.tensor_tensor(diagonal, diagonal,
                                  causal_add[:].unsqueeze(1).unsqueeze(1).to_broadcast([P, HEADS, 2, P]), ALU.add))
            split(1)

            dve.wait_ge(gated_x_ready, 1)
            dve.wait_ge(decay_exp_ready, 1)
            dve.wait_ge(decay_tanh_ready, 2)
            chain(v.scalar_tensor_tensor(c_[:], a[:], 1.0, c_[:], ALU.add, ALU.mult))
            chain(v.tensor_scalar(d_[:], c_[:], 1.0, None, ALU.add))
            split(1)
            chain(v.tensor_tensor(a[:], d_[:], d_[:], ALU.mult))
            v.scalar_tensor_tensor(a[:], a[:], 1.0, f_[:], ALU.add, ALU.mult).then_inc(rest_ready, 1)
            split(1)
            chain(v.tensor_tensor(c_[:], b_[:], b_[:], ALU.mult))
            split(1)
            chain(v.tensor_scalar(c_[:], c_[:], 0.044715, 1.0, ALU.mult, ALU.add))
            chain(v.tensor_tensor(c_[:], c_[:], b_[:], ALU.mult))
            split(1)
            dve.wait_ge(root_ready, 1)
            v.scalar_tensor_tensor(e_[:], e_[:], 0.5, f_[:], ALU.mult, ALU.mult).then_inc(gelu_in_ready, 1)
            dve.wait_ge(gelu_in_ready, 1)
            dve.wait_ge(rest_ready, 1)
            split(1)
            for n in range(HEADS):
                did(v.tensor_tensor_scan(a[:, n], d_[:, n], e_[:, n], 0.0, ALU.mult, ALU.add))
                if n == 1:
                    split(1)
            settle()
            split(1)
            dve.wait_ge(gelu_tanh_ready, 1)
            chain(v.scalar_tensor_tensor(c_[:], f_[:], 1.0, b_[:], ALU.add, ALU.mult))
            v.scalar_tensor_tensor(c_[:], c_[:], 0.5, a[:], ALU.mult, ALU.mult).then_inc(lru_out_ready, 1)
            split(2)
            dve.wait_ge(lru_out_ready, 1)
            dve.wait_ge(evac_hi, hi_in.next())
            v.tensor_sub(oT_lo[:, 1], c_[:], oT_hi[:, 1]).then_inc(branch_done, 1)
            split(2)
            for _ in range(2):
                skip_job(0)
                skip_job(1)

            exps = Count(exp_ready)
            logs = Count(stick_log_ready)

            def softmax_logits(h, bias0, bias1):
                wait_job(0)
                p = logits[:, h % 2]
                did(v.scalar_tensor_tensor(p[:, 0:P], aux[0][:, 0:P], SCALE, bias0, ALU.mult, ALU.add))
                v.scalar_tensor_tensor(p[:, P:3 * P], aux[0][:, P:3 * P], SCALE, bias1,
                                       ALU.mult, ALU.add).then_inc(aux_taken[0], 1)
                settle()
                dve.wait_ge(aux_taken[0], job[0].value())
                did(v.tensor_reduce(peak[:, 0:1], p[:, 0:P], AX.X, ALU.max))
                chain(v.tensor_reduce(peak[:, 1:2], p[:, P:3 * P], AX.X, ALU.max))
                v.tensor_scalar(neg_peak[:], peak[:], -1.0, None, ALU.mult).then_inc(peak_ready, 1)

            def softmax_scale(h):
                dve.wait_ge(exp_ready, exps.next())
                p = logits[:, h % 2]
                chain(v.reciprocal(inv_total[:], total[:]))
                did(v.tensor_scalar(p[:, 0:P], p[:, 0:P], inv_total[:, 0:1], None, ALU.mult))
                v.tensor_scalar(p[:, P:3 * P], p[:, P:3 * P], inv_total[:, 1:2], None, ALU.mult).then_inc(probs_ready, 1)

            def stick_relu(h):
                wait_job(0)
                dve.wait_ge(stick_log_ready, logs.next())
                chain(v.tensor_scalar(stick_b[:], aux[0][:, 0:3 * P], SCALE, 0.0, ALU.mult, ALU.max))

            def stick_logits(h):
                chain(v.scalar_tensor_tensor(stick_b[:], stick_b[:], -1.0, stick_l[:], ALU.mult, ALU.subtract))
                diag = stick_b[:].rearrange("p (c k) -> p c k", k=P)[:, 0::2, :]
                chain(v.tensor_tensor(diag, diag, strict_mul[:].unsqueeze(1).to_broadcast([P, 2, P]), ALU.mult))
                did(v.tensor_tensor_scan(stick_c[:, P - 1::-1], ones[:, 0:P], stick_b[:, P - 1::-1], 0.0, ALU.mult, ALU.add))
                chain(v.tensor_tensor_scan(stick_c[:, 3 * P - 1:P - 1:-1], ones[:], stick_b[:, 3 * P - 1:P - 1:-1],
                                           0.0, ALU.mult, ALU.add))
                p = logits[:, h % 2]
                v.scalar_tensor_tensor(p, aux[0][:, 0:3 * P], SCALE, stick_c[:], ALU.mult, ALU.add).then_inc(aux_taken[0], 1)
                dve.wait_ge(aux_taken[0], job[0].value())
                diag = p.rearrange("p (c k) -> p c k", k=P)[:, 0::2, :]
                v.tensor_tensor(diag, diag, strict_add[:].unsqueeze(1).to_broadcast([P, 2, P]),
                                ALU.add).then_inc(stick_logits_ready, 1)

            def mixed_out(branch, h):
                wait_job(1)
                dve.wait_ge(evac_hi, hi_in.next())
                v.tensor_sub(oT_lo[:, branch, h, :], aux[1][:, 0:SEQ], oT_hi[:, branch, h, :]).then_inc(aux_taken[1], 1)

            def attention_step(branch, step):
                h = step // 3
                if step % 3 == 0 and 1 <= h <= HEADS:
                    skip_job(1)
                if step % 3 == 1 and 1 <= h <= HEADS:
                    mixed_out(branch, h - 1)
                if h >= HEADS:
                    return
                if branch == 2:
                    if step % 3 == 1:
                        stick_relu(h)
                        stick_logits(h)
                else:
                    if step % 3 == 0 and branch == 0:
                        softmax_logits(h, fox_bias[:, h, 0:P], fox_bias[:, h, P:3 * P])
                    if step % 3 == 0 and branch == 3:
                        softmax_logits(h, band_bias[:, h, P - 1::-1], band_bias[:, h, SEQ - 1::-1])
                    if step % 3 == 2:
                        softmax_scale(h)

            for branch in (0, 2):
                for step in range(3 * SLABS):
                    attention_step(branch, step)
                    split(1)
                    if step in (14, 18):
                        skip_job(0)
                        skip_job(1)
                    if branch == 0 and step == 11:
                        v.memset(band_bias[0:CHUNK, :, 0:CHUNK], MASKED).then_inc(rel_mask_ready, 1)

            gates = Count(gate_ready)
            biases = Count(gate_bias_loaded[0])

            def merge_row(first, n=None):
                for step in range(ROW_STEPS):
                    g, s = divmod(step, GATE_STEPS)
                    if first:
                        if step == 0:
                            dve.wait_ge(rel_loaded, 32)
                            dve.wait_ge(rel_mask_ready, 1)
                        attention_step(3, step)
                    elif step == 2:
                        for b in range(2):
                            wait_job(b)
                            dve.wait_ge(evac_hi, hi_in.next())
                            k = n * (NC // P) + 2 * b
                            v.scalar_tensor_tensor(zT_lo[:, bass.ds(k, 2), :], aux[b][:].rearrange("p (k t) -> p k t", k=2),
                                                   0.5, zT_hi[:, bass.ds(k, 2), :], ALU.mult, ALU.subtract).then_inc(aux_taken[b], 1)
                    split(1)
                    if s == SLABS - 1:
                        dve.wait_ge(slab_used, slab.value(LEAD))
                        dve.wait_ge(gate_bias_loaded[g % 2], biases.scaled(16, 2) + 16)
                        biases.next()
                        v.tensor_tensor(gate[:, 0], acc[g % 2][0][:], b_gate_rows[:, g % 2], ALU.add)
                        v.tensor_tensor(gate[:, 1], acc[g % 2][1][:], b_gate_rows[:, g % 2], ALU.add).then_inc(gate_in_ready, 1)
                    if s == GATE_STEPS - 1:
                        dve.wait_ge(slab_used, slab.value(LEAD))
                        dve.wait_ge(gate_ready, gates.next())
                        for t in range(TT):
                            to = stage if g == 0 else gate
                            ins = v.scalar_tensor_tensor(to[:, t], gate[:, t], 1.0, acc[2][t][:], ALU.add, ALU.mult)
                        ins.then_inc(mix_taken, 1)
                        mixed.next()
                        if g:
                            dve.wait_ge(mix_taken, mixed.value())
                            ins = v.tensor_tensor(stage[:], stage[:], gate[:], ALU.add)
                            if g == 3:
                                ins.then_inc(merged_ready, 1)
                            else:
                                did(ins)
                                settle()

            mixed = Count(mix_taken)
            merge_row(True)
            with loop(dve, CB - 1, {slab: ROW_STEPS, job[0]: 1, job[1]: 1, hi_in: 2, gates: 4, biases: 4,
                                    mixed: 4, done: 2}) as n:
                merge_row(False, n)

            split(3)
            for b in range(2):
                wait_job(b)
                dve.wait_ge(evac_hi, hi_in.next())
                k = (CB - 1) * (NC // P) + 2 * b
                v.scalar_tensor_tensor(zT_lo[:, k:k + 2, :], aux[b][:].rearrange("p (k t) -> p k t", k=2),
                                       0.5, zT_hi[:, k:k + 2, :], ALU.mult, ALU.subtract).then_inc(aux_taken[b], 1)
            def accumulate(t, m, factor):
                cols = slice(m * NC, (m + 1) * NC)
                chain(v.scalar_tensor_tensor(x_tok[:, t, cols], x_tok[:, t, cols], factor, acc[m % 2][t][:], ALU.mult, ALU.add))
                statistics(t, m)

            def give_back():
                ins = v.memset(neg_peak[:], 0.0)
                ins.then_inc(acc_taken, 1)
                acc_done.next()

            rows0 = Count(row0_ready)
            dve.wait_ge(residual_ready, 1)
            for m in range(CB - 1):
                split(SLABS - 3 if m == 0 else SLABS)
                dve.wait_ge(slab_used, slab.value(LEAD))
                for t in range(TT):
                    accumulate(t, m, ALPHA)
                give_back()
            split(LEAD)
            dve.wait_ge(row0_ready, rows0.next())
            accumulate(0, CB - 1, ALPHA)
            spread(0)
            normalise(0)
            split(LEAD - 1)
            dve.wait_ge(slab_used, slab.value(LEAD - 1))
            accumulate(1, CB - 1, ALPHA)
            give_back()
            spread(1)
            normalise(1)
            split(1)
            normed_pair(0)
            normed_pair(1)
            relus = Count(relu_ready)

            def hidden(pair):
                dve.wait_ge(relu_ready, relus.next())
                for t in range(TT):
                    ins = v.tensor_tensor(stage[:, t], acc[pair][t][:], stage[:, t], ALU.mult)
                ins.then_inc(acc_taken, 1)
                acc_done.next()

            for s in range(SLABS):
                if s + 2 < SLABS:
                    normed_pair(s + 2)
                split(1)
            hidden(0)

            with loop(dve, QUARTERS, {relus: CB, slab: QUARTER_STEPS, job[0]: CB, job[1]: CB, hi_in: 2 * CB,
                                      acc_done: 2 * CB, rows0: 1, done: 4 * CB + 1}) as q:
                for step in range(SLABS, QUARTER_STEPS - LEAD):
                    i, s = divmod(step, SLABS)
                    if s == 2 and i <= CB:
                        for b in range(2):
                            wait_job(b)
                            dve.wait_ge(evac_hi, hi_in.next())
                            k = (i - 1) * (NC // P) + 2 * b
                            v.tensor_sub(zT_lo[:, k:k + 2, :], aux[b][:].rearrange("p (k t) -> p k t", k=2),
                                         zT_hi[:, k:k + 2, :]).then_inc(aux_taken[b], 1)
                    split(1)
                    if s == SLABS - 1:
                        if i < CB:
                            hidden(i % 2)
                        else:
                            dve.wait_ge(slab_used, slab.value(LEAD))
                            if i == CB:
                                dve.wait_ge(residual_ready, 2)
                            for t in range(TT):
                                accumulate(t, i - CB, carry[:])
                            give_back()
                dve.wait_ge(row0_ready, rows0.next())
                accumulate(0, CB - 1, carry[:])
                with dve.If(QUARTERS - 1 - q):
                    split(LEAD - 1)
                dve.wait_ge(slab_used, slab.value(LEAD - 1))
                accumulate(1, CB - 1, carry[:])
                give_back()
                did(v.memset(carry[:], 1.0))
                with dve.If(QUARTERS - 1 - q):
                    split(SLABS + 1)
                    hidden(0)

            for t in range(TT):
                spread(t)
            for t in range(TT):
                dve.wait_ge(std_ready, std.next())
                chain(v.reciprocal(rstd[:, t:t + 1], rstd[:, t:t + 1]))
            v.memset(neg_peak[:], 0.0).then_inc(inv_ready, 1)
            dve.wait_ge(norm_loaded, 96)
            for t in range(TT):
                for m in range(CB):
                    cols = slice(m * NC, (m + 1) * NC)
                    ins = v.scalar_tensor_tensor(x_tok[:, t, cols], x_tok[:, t, cols], mean_var[:, t, 0:1],
                                                 norm_rows[:, 0, cols], ALU.subtract, ALU.mult)
                    if t == 0:
                        ins.then_inc(gained_ready, 1)
                    else:
                        chain(ins)
                        v.scalar_tensor_tensor(x_tok[:, t, cols], x_tok[:, t, cols], rstd[:, t:t + 1],
                                               norm_rows[:, 1, cols], ALU.mult, ALU.add).then_inc(y1_ready, 1)

        @block.gpsimd
        def _(pool):
            g = nc.gpsimd
            for tile, value in ((ident, 0.0), (ones, 1.0), (causal_add, 0.0), (strict_add, 0.0),
                                (strict_mul, 1.0)):
                ins = g.memset(tile[:], value)
            ins.then_inc(pool_done, 1)
            pool.wait_ge(pool_done, 1)
            g.affine_select(out=ident[:], in_=ident[:], compare_op=ALU.not_equal, fill=1.0, base=0,
                            pattern=[[-1, P]], channel_multiplier=1)
            g.affine_select(out=causal_add[:], in_=causal_add[:], compare_op=ALU.is_ge, fill=MASKED, base=0,
                            pattern=[[-1, P]], channel_multiplier=1)
            g.affine_select(out=strict_add[:], in_=strict_add[:], compare_op=ALU.is_ge, fill=MASKED, base=-1,
                            pattern=[[-1, P]], channel_multiplier=1)
            g.affine_select(out=strict_mul[:], in_=strict_mul[:], compare_op=ALU.is_ge, fill=0.0, base=-1,
                            pattern=[[-1, P]], channel_multiplier=1).then_inc(consts_ready, 1)
            pool.wait_ge(norm_loaded, 32)
            for t in range(TT):
                ins = g.tensor_tensor(x_tok[:, t], x_tok[:, t], norm_rows[:, 0], ALU.mult)
            ins.then_inc(pool_done, 1)
            pool.wait_ge(pool_done, 2)
            for t in range(TT):
                ins = g.tensor_tensor(x_tok[:, t], x_tok[:, t], norm_rows[:, 1], ALU.add)
            ins.then_inc(residual_ready, 1)
            pool.wait_ge(norm_loaded, 64)
            for b in range(2):
                pool.wait_ge(aux_ready[b], mark["x1_transposed"][b])
            for t in range(TT):
                ins = g.tensor_tensor(x_tok[:, t], x_tok[:, t], norm_rows[:, 0], ALU.mult)
            ins.then_inc(pool_done, 1)
            pool.wait_ge(pool_done, 3)
            for t in range(TT):
                ins = g.tensor_tensor(x_tok[:, t], x_tok[:, t], norm_rows[:, 1], ALU.add)
            ins.then_inc(residual_ready, 1)
            for m in range(CB):
                cols = slice(m * NC, (m + 1) * NC)
                pool.wait_ge(scaled_ready, m + 1)
                g.tensor_tensor(x_tok[:, 0, cols], x_tok[:, 0, cols], norm_rows[:, 1, cols],
                                ALU.add).then_inc(y_ready, 1)

        @block.sync
        def _(sp):
            slab = Count(lo_ready)
            biases = Count(gate_in_ready)

            def load_slab(view):
                slot = slab.n % RING
                if slab.n >= RING:
                    sp.wait_ge(lo_ready, slab.value(RING - 1))
                sp.dma_start(w_raw[:, slot], view.rearrange("(k p) n -> p k n", p=P)).then_inc(slab_loaded[slot], 16)
                slab.next()

            def load_group(w, col, slabs=SLABS):
                for s in range(slabs):
                    load_slab(w[s * SLAB_K * P:(s + 1) * SLAB_K * P, bass.ds(col, NC)])

            def load_norm(gain, shift):
                sp.dma_start(norm_rows[:, 0], gain.partition_broadcast(P)).then_inc(norm_loaded, 16)
                sp.dma_start(norm_rows[:, 1], shift.partition_broadcast(P)).then_inc(norm_loaded, 16)

            for t in range(TT):
                sp.dma_start(x_tok[:, t, :], x[0, t * P:(t + 1) * P, :]).then_inc(x_loaded[t], 16)
            for j in range(2):
                load_group(w_in[0], LRU + j * NC)
            with loop(sp, 3, {slab: SLABS}) as j:
                load_group(w_in[0], FOX + j * NC)
            with loop(sp, 6, {slab: SLABS}) as j:
                load_group(w_in[0], STICK + j * NC)
            rel = rel_bias[0]
            sp.wait_ge(rel_mask_ready, 1)
            for half, first in ((0, CHUNK), (1, 0)):
                src = bass.AP(rel.tensor, rel.offset, [[1, CHUNK], [REL, HEADS], [1, SEQ - first]])
                sp.dma_start(band_bias[half * CHUNK:(half + 1) * CHUNK, :, first:], src).then_inc(rel_loaded, 16)

            def load_merge_row(col, first):
                for g in range(4):
                    if not first or g >= 2:
                        sp.wait_ge(gate_in_ready, biases.value(1))
                    sp.dma_start(b_gate_rows[:, g % 2], b_gate[0][g, bass.ds(col, NC)].partition_broadcast(P)
                                 ).then_inc(gate_bias_loaded[g % 2], 16)
                    biases.next()
                    load_group(w_gate[0][g], col)
                    load_group(w_branch[0][g], col, MIX_SLABS)

            load_merge_row(0, True)
            sp.wait_ge(aux_taken[1], mark["attention_done"])
            load_norm(ln_in_g, ln_in_b)
            with loop(sp, CB - 1, {slab: ROW_STEPS, biases: 4}) as n:
                load_merge_row(n * NC + NC, False)
            sp.wait_ge(residual_ready, 1)
            load_norm(ln1_g[0], ln1_b[0])
            with loop(sp, CB, {slab: SLABS}) as m:
                load_group(w_out[0], m * NC)
            with loop(sp, QUARTERS, {slab: QUARTER_STEPS}) as q:
                with loop(sp, CB, {slab: SLABS}) as i:
                    load_group(w_ff1[0], q * D + i * NC)
                with loop(sp, CB, {slab: SLABS}) as m:
                    for s in range(SLABS):
                        load_slab(w_ff2[0][bass.ds(q * D + s * SLAB_K * P, SLAB_K * P), bass.ds(m * NC, NC)])
            sp.wait_ge(residual_ready, 2)
            load_norm(ln2_g[0], ln2_b[0])
            for t, ready in enumerate((y_ready, y1_ready)):
                for m in range(CB):
                    cols = slice(m * NC, (m + 1) * NC)
                    sp.wait_ge(ready, m + 1)
                    sp.dma_start(out[0, t * P:(t + 1) * P, cols], x_tok[:, t, cols]).then_inc(out_stored, 16)
            sp.wait_ge(out_stored, 16 * TT * CB)


INPUTS = ["x", "ln_in_g", "ln_in_b", "w_in", "b_forget", "conv_w", "conv_b", "w_r", "b_r", "w_i", "b_i", "lru_lambda",
          "rel_bias", "w_branch", "w_gate", "b_gate", "w_out", "ln1_g", "ln1_b", "w_ff1", "w_ff2", "ln2_g", "ln2_b"]


def kernel(**inputs):
    import numpy as np
    import concourse.bacc as bacc
    from concourse.bass_utils import run_bass_kernel_spmd

    nc = bacc.Bacc("TRN2", target_bir_lowering=False, num_devices=1)
    arrays, args = {}, []
    for name in INPUTS:
        a = np.ascontiguousarray(inputs[name])
        arrays[f"in_{name}"] = a
        args.append(nc.dram_tensor(f"in_{name}", a.shape, mybir.dt.from_np(a.dtype), kind="ExternalInput").ap())
    args.append(nc.dram_tensor("out_x", (1, SEQ, D), F32, kind="ExternalOutput").ap())
    build(nc, *args)
    return run_bass_kernel_spmd(nc, [arrays], core_ids=[0]).results[0]["out_x"]
```

```python
from contextlib import ExitStack, contextmanager

import concourse.bass as bass
from concourse import mybir

F32 = mybir.dt.float32
F32R = mybir.dt.float32r
ALU = mybir.AluOpType
ACT = mybir.ActivationFunctionType
AX = mybir.AxisListType

P = 128
SEQ = 256
TT = SEQ // P
D = 2048
KT = D // P
NC = 512
CB = D // NC
HEADS = 4
CHUNK = 64
REL = 256 + CHUNK
CONV = 4
FF = 4 * D
SLAB_K = 2
SLABS = KT // SLAB_K
MIX_SLABS = NC // P // SLAB_K
RING = 4
LEAD = RING
IN_GROUPS = 11
QUARTERS = FF // D
GATE_STEPS = SLABS + MIX_SLABS
ROW_STEPS = 4 * GATE_STEPS
QUARTER_STEPS = 2 * CB * SLABS
SHARED = 2
ALPHA = 2.0 ** 0.25
SCALE = P ** -0.5
EPS = 1e-5
MASKED = -1e30
GELU_C = (2.0 / 3.141592653589793) ** 0.5
FOX, FORGET, LRU, STICK = 0, 3 * NC, 3 * NC + HEADS, 5 * NC + HEADS
LN_IN_G, LN_IN_B, LN1_G, LN1_B, CONV_W, CONV_B, B_R, B_I, LAM = 0, 16, 32, 48, 64, 80, 84, 88, 92
PARAMS = 96


class Count:

    def __init__(self, sem, start=0):
        self.sem, self.n, self.loops = sem, start, []

    def value(self, back=0):
        v = self.n - back
        for turn, per, _ in self.loops:
            v = turn * per + v
        return v

    def scaled(self, num, den):
        v = self.n // den * num
        for turn, per, _ in self.loops:
            assert per % den == 0
            v = turn * (per // den * num) + v
        return v

    def next(self, k=1):
        self.n += k
        return self.value()


@contextmanager
def loop(eng, trips, per):
    with eng.Fori(0, trips) as turn:
        for c, k in per.items():
            c.loops.append((turn, k, c.n))
        yield turn
        for c, k in per.items():
            _, _, start = c.loops.pop()
            assert c.n - start == k, (c.sem, c.n - start, k)
            c.n = start + k * trips


def build(nc, x, ln_in_g, ln_in_b, w_in, b_forget, conv_w, conv_b, w_r, b_r, w_i, b_i, lru_lambda,
          rel_bias, w_branch, w_gate, b_gate, w_out, ln1_g, ln1_b, w_ff1, w_ff2, ln2_g, ln2_b, out):
    with ExitStack() as ctx:
        top = [(nc.sbuf_base + 63) // 64 * 64]
        def place(name, shape, dtype=F32, at=None):
            size = 4
            for n in shape[1:]:
                size *= n
            if at is None:
                at = top[0]
                top[0] += (size + 63) // 64 * 64
            return nc.alloc_sbuf_tensor_at(name, shape, dtype, offset=at), at

        x_tok, _ = place("x_tok", [P, TT, D])
        xT_hi, _ = place("xT_hi", [P, KT, SEQ], F32R)
        xT_lo, _ = place("xT_lo", [P, KT, SEQ], F32R)
        zT_hi, z_at = place("zT_hi", [P, KT, SEQ], F32R)
        zT_lo, _ = place("zT_lo", [P, KT, SEQ], F32R)
        oT_hi, o_at = place("oT_hi", [P, 4, HEADS, SEQ], F32R)
        oT_lo, _ = place("oT_lo", [P, 4, HEADS, SEQ], F32R)
        w_raw, _ = place("w_raw", [P, RING, SLAB_K, NC])
        w_hi, _ = place("w_hi", [P, RING, SLAB_K, NC], F32R)
        w_lo, _ = place("w_lo", [P, RING, SLAB_K, NC], F32R)
        stage, _ = place("stage", [P, TT, NC])
        gate, _ = place("gate", [P, TT, NC])
        b_gate_rows, _ = place("b_gate_rows", [P, 2, NC])
        qT, att_at = place("qT", [P, HEADS, SEQ])
        kT, _ = place("kT", [P, HEADS, SEQ])
        v_tok, v_at = place("v_tok", [P, TT, NC])
        logits, logits_at = place("logits", [P, 2, 3 * P])
        stick_l, _ = place("stick_l", [P, 3 * P])
        stick_b, _ = place("stick_b", [P, 3 * P])
        stick_c, _ = place("stick_c", [P, 3 * P])
        probsT, probsT_at = place("probsT", [P, 3 * P])
        fox_bias, bias_at = place("fox_bias", [P, HEADS, 3 * P])
        band_bias, _ = place("band_bias", [P, HEADS, SEQ], at=bias_at)
        lru = [place(f"lru_{c}", [P, HEADS, SEQ], at=z_at + 4096 * i)[0] for i, c in enumerate("abcdef")]
        w_ri, _ = place("w_ri", [P, 2, HEADS, P], at=v_at)
        sig, _ = place("sig", [P, 6, SEQ + HEADS], at=logits_at)
        param_rows, _ = place("param_rows", [P, P], at=probsT_at)
        wf_hi, _ = place("wf_hi", [P, KT, P], F32R, at=o_at)
        wf_lo, _ = place("wf_lo", [P, KT, P], F32R, at=o_at + 4 * KT * P)
        norm_rows, _ = place("norm_rows", [P, 2, D], at=att_at)
        ident, _ = place("ident", [P, P])
        ones, _ = place("ones", [P, SEQ])
        causal_add, _ = place("causal_add", [P, P])
        strict_add, _ = place("strict_add", [P, P])
        strict_mul, _ = place("strict_mul", [P, P])
        params, _ = place("params", [P, PARAMS])
        wf_raw, _ = place("wf_raw", [P, KT, HEADS])
        bn, _ = place("bn", [P, TT, CB, 6])
        mean_var, _ = place("mean_var", [P, TT, 2])
        rstd, _ = place("rstd", [P, TT])
        peak, _ = place("peak", [P, 2])
        neg_peak, _ = place("neg_peak", [P, 2])
        total, _ = place("total", [P, 2])
        inv_total, _ = place("inv_total", [P, 2])
        b_forget_col, _ = place("b_forget_col", [P, 1])
        carry, _ = place("carry", [P, 1])
        first_root, _ = place("first_root", [P, 1])
        cum_q, _ = place("cum_q", [P, TT, HEADS])
        lru_cols, _ = place("lru_cols", [P, 4, HEADS])
        assert top[0] <= nc.sbuf_usable_end, (top[0], nc.sbuf_usable_end)

        def psum(name):
            return ctx.enter_context(nc.psum_tensor(name, [P, NC], F32))
        acc = [[psum(f"acc{i}{t}") for t in range(TT)] for i in range(3)]
        aux = [psum("aux0"), psum("aux1")]

        def sem(name):
            return ctx.enter_context(nc.semaphore(name))
        x_loaded = [[sem(f"x_loaded{t}_{m}") for m in range(CB)] for t in range(TT)]
        params_loaded = sem("params_loaded")
        small_loaded = sem("small_loaded")
        slab_loaded = [sem(f"slab_loaded{i}") for i in range(RING)]
        rel_loaded = sem("rel_loaded")
        gate_bias_loaded = [sem("gate_bias_loaded0"), sem("gate_bias_loaded1")]
        norm_loaded = sem("norm_loaded")
        out_stored = sem("out_stored")
        consts_ready = sem("consts_ready")
        hi_ready = sem("hi_ready")
        lo_ready = sem("lo_ready")
        slab_used = sem("slab_used")
        acc_taken = sem("acc_taken")
        aux_ready = [sem("aux_ready0"), sem("aux_ready1")]
        aux_taken = [sem("aux_taken0"), sem("aux_taken1")]
        var_ready = sem("var_ready")
        std_ready = sem("std_ready")
        xn_ready = sem("xn_ready")
        xn_rest_ready = sem("xn_rest_ready")
        evac_hi = sem("evac_hi")
        wf_hi_ready = sem("wf_hi_ready")
        wf_ready = sem("wf_ready")
        u_taken = sem("u_taken")
        sig_in = sem("sig_in")
        sig_exp = sem("sig_exp")
        cum_ready = sem("cum_ready")
        row0_ready = sem("row0_ready")
        normed_ready = sem("normed_ready")
        conv_ready = sem("conv_ready")
        lru_cols_ready = sem("lru_cols_ready")
        gated_x_ready = sem("gated_x_ready")
        decay_exp_ready = sem("decay_exp_ready")
        decay_tanh_ready = sem("decay_tanh_ready")
        rest_ready = sem("rest_ready")
        root_ready = sem("root_ready")
        gelu_in_ready = sem("gelu_in_ready")
        gelu_tanh_ready = sem("gelu_tanh_ready")
        lru_out_ready = sem("lru_out_ready")
        branch_done = sem("branch_done")
        peak_ready = sem("peak_ready")
        exp_ready = sem("exp_ready")
        probs_ready = sem("probs_ready")
        stick_log_ready = sem("stick_log_ready")
        stick_logits_ready = sem("stick_logits_ready")
        rel_mask_ready = sem("rel_mask_ready")
        gate_in_ready = sem("gate_in_ready")
        gate_ready = sem("gate_ready")
        mix_taken = sem("mix_taken")
        merged_ready = sem("merged_ready")
        relu_ready = sem("relu_ready")
        residual_ready = sem("residual_ready")
        act_done = sem("act_done")
        dve_done = sem("dve_done")
        pool_done = sem("pool_done")
        pool_rows_ready = sem("pool_rows_ready")
        gained_ready = sem("gained_ready")
        inv_ready = sem("inv_ready")
        scaled_ready = sem("scaled_ready")
        dve_rows_ready = sem("dve_rows_ready")

        PARAM_ROWS = [(ln_in_g, LN_IN_G), (ln_in_b, LN_IN_B), (ln1_g[0], LN1_G), (ln1_b[0], LN1_B),
                      (conv_w[0].rearrange("j c -> (j c)"), CONV_W), (conv_b[0], CONV_B), (b_r[0], B_R),
                      (b_i[0], B_I), (lru_lambda[0], LAM)]

        def load_params(eng, vec, at):
            n = vec.shape[0] // P
            eng.dma_start(param_rows[at:at + n, :], vec.rearrange("(k p) -> k p", p=P)).then_inc(params_loaded, 16)

        def repeated(tile):
            return tile.rearrange("p k (r h) -> p k r h", h=HEADS)
        wf_wide = wf_raw[:].unsqueeze(2).to_broadcast([P, KT, P // HEADS, HEADS])

        block = ctx.enter_context(nc.Block())
        mark = {}

        @block.tensor
        def _(pe):
            slab = Count(slab_used)
            job = [Count(aux_taken[0]), Count(aux_taken[1])]
            projected = Count(u_taken)
            gated = Count(gate_in_ready)
            groups = Count(acc_taken)

            def free(b):
                if job[b].n:
                    pe.wait_ge(aux_taken[b], job[b].value())
                job[b].next()

            def start_projection():
                if projected.n >= 2:
                    pe.wait_ge(u_taken, projected.value(1))
                projected.next()

            def start_gate():
                if gated.n >= 2:
                    pe.wait_ge(gate_in_ready, gated.value(1))
                else:
                    pe.wait_ge(u_taken, IN_GROUPS - 1)
                gated.next()

            def start_group():
                if groups.n >= 2:
                    pe.wait_ge(acc_taken, groups.value(1))
                else:
                    pe.wait_ge(gate_in_ready, gated.value(1 - groups.n))
                groups.next()

            def products(pair, hi, lo, slabs, first, last):
                for s in slabs:
                    slot = slab.n % RING
                    slab.next()
                    pe.wait_ge(lo_ready, slab.value())
                    for kk in range(SLAB_K):
                        k = s * SLAB_K + kk
                        for t in range(TT):
                            toks = slice(t * P, (t + 1) * P)
                            begin = s == first and kk == 0
                            end = s == last and kk == SLAB_K - 1
                            nc.tensor.matmul(acc[pair][t][:], hi[:, k, toks], w_hi[:, slot, kk], start=begin, stop=False)
                            nc.tensor.matmul(acc[pair][t][:], hi[:, k, toks], w_lo[:, slot, kk], start=False, stop=False)
                            mm = nc.tensor.matmul(acc[pair][t][:], lo[:, k, toks], w_hi[:, slot, kk], start=False, stop=end)
                    mm.then_inc(slab_used, 1)

            def tile_products(pair, t, hi, lo, s, slot, first, last):
                for kk in range(SLAB_K):
                    k = s * SLAB_K + kk
                    toks = slice(t * P, (t + 1) * P)
                    begin = s == first and kk == 0
                    end = s == last and kk == SLAB_K - 1
                    nc.tensor.matmul(acc[pair][t][:], hi[:, k, toks], w_hi[:, slot, kk], start=begin, stop=False)
                    nc.tensor.matmul(acc[pair][t][:], hi[:, k, toks], w_lo[:, slot, kk], start=False, stop=False)
                    mm = nc.tensor.matmul(acc[pair][t][:], lo[:, k, toks], w_hi[:, slot, kk], start=False, stop=end)
                return mm

            def rows_apart(pair, hi, lo, slabs, last, beside=None):
                slots = []
                for s in slabs:
                    slots.append(slab.n % RING)
                    slab.next()
                for t in range(TT):
                    for n, s in enumerate(slabs):
                        if t == 0:
                            pe.wait_ge(lo_ready, slab.value(len(slabs) - 1 - n))
                        mm = tile_products(pair, t, hi, lo, s, slots[n], None, last)
                        if t == 1:
                            mm.then_inc(slab_used, 1)
                            if beside and n == len(slabs) - 2:
                                beside()
                        elif s == last:
                            mm.then_inc(row0_ready, 1)

            def slabs_of(pair, hi, lo, slabs, total=SLABS):
                products(pair, hi, lo, slabs, 0, total - 1)

            def transpose_tokens(pair):
                b = pair % 2
                free(b)
                for kk in range(2):
                    k = 2 * pair + kk
                    for t in range(TT):
                        mm = nc.tensor.transpose(aux[b][:, kk * SEQ + t * P:kk * SEQ + (t + 1) * P],
                                                 x_tok[:, t, k * P:(k + 1) * P], ident[:])
                mm.then_inc(aux_ready[b], 1)

            def transpose_stage():
                for b in range(2):
                    free(b)
                    for kk in range(2):
                        k = 2 * b + kk
                        for t in range(TT):
                            mm = nc.tensor.transpose(aux[b][:, kk * SEQ + t * P:kk * SEQ + (t + 1) * P],
                                                     stage[:, t, k * P:(k + 1) * P], ident[:])
                    mm.then_inc(aux_ready[b], 1)

            def transpose_projected():
                pe.wait_ge(u_taken, projected.value(1))
                transpose_stage()

            def transpose_hidden(back):
                pe.wait_ge(acc_taken, groups.value(back))
                transpose_stage()

            def keep_warm(n):
                for _ in range(n):
                    nc.tensor.matmul(acc[2][0][:, 0:SEQ], ident[:], ones[:], start=True, stop=True)

            pe.wait_ge(consts_ready, 1)
            keep_warm(12)
            pe.wait_ge(params_loaded, 16 * 9)
            free(0)
            nc.tensor.transpose(aux[0][:, 0:PARAMS], param_rows[0:PARAMS, :],
                                ident[0:PARAMS, 0:PARAMS]).then_inc(aux_ready[0], 1)
            keep_warm(4)
            normed = Count(normed_ready)

            def transpose_tile(t, norm):
                for b in range(2):
                    transpose_quarter(t, b, norm)

            def transpose_quarter(t, b, norm):
                pe.wait_ge(xn_ready, 2 * TT * norm + 2 * t + b + 1)
                free(b)
                for kk in range(4):
                    k = 4 * b + kk
                    mm = nc.tensor.transpose(aux[b][:, kk * P:(kk + 1) * P], x_tok[:, t, k * P:(k + 1) * P], ident[:])
                mm.then_inc(aux_ready[b], 1)

            def first_group(start, norm):
                start()
                slots = []
                for s in range(SLABS // 2):
                    slots.append(slab.n % RING)
                    slab.next()
                    pe.wait_ge(lo_ready, slab.value())
                    if s % 2 == 0:
                        pe.wait_ge(normed_ready, normed.next())
                    tile_products(0, 0, xT_hi, xT_lo, s, slots[s], 0, None)
                    if s in (1, 2):
                        transpose_quarter(1, s - 1, norm)
                for s in range(SLABS // 2):
                    if s % 2 == 0:
                        pe.wait_ge(normed_ready, normed.next())
                    tile_products(0, 1, xT_hi, xT_lo, s, slots[s], 0, None).then_inc(slab_used, 1)
                    if s == 1:
                        pe.wait_ge(xn_rest_ready, TT * norm + TT)
                    if s:
                        transpose_tokens(s + 3)
                for s in range(SLABS // 2, SLABS):
                    pe.wait_ge(normed_ready, normed.next())
                    slabs_of(0, xT_hi, xT_lo, [s])
                    if s + 3 < SLABS:
                        transpose_tokens(s + 3)

            transpose_tile(0, 0)
            keep_warm(5)
            first_group(start_projection, 0)

            start_projection()
            slabs_of(1, xT_hi, xT_lo, [0, 1, 2])
            transpose_projected()
            slabs_of(1, xT_hi, xT_lo, [3])
            free(0)
            pe.wait_ge(wf_ready, 1)
            for k in range(KT):
                nc.tensor.matmul(aux[0][:, 0:SEQ], wf_hi[:, k], xT_hi[:, k], start=k == 0, stop=False)
                nc.tensor.matmul(aux[0][:, 0:SEQ], wf_hi[:, k], xT_lo[:, k], start=False, stop=False)
                mm = nc.tensor.matmul(aux[0][:, 0:SEQ], wf_lo[:, k], xT_hi[:, k], start=False, stop=k == KT - 1)
            mm.then_inc(aux_ready[0], 1)
            slabs_of(1, xT_hi, xT_lo, [4, 5, 6, 7])

            def recurrent_gate(which):
                for b in range(2):
                    free(b)
                    for hh in range(2):
                        n = 2 * b + hh
                        mm = nc.tensor.matmul(aux[b][:, hh * SEQ:(hh + 1) * SEQ], w_ri[:, which, n],
                                              lru[2][:, n, :], start=True, stop=True)
                    mm.then_inc(aux_ready[b], 1)

            start_projection()
            slabs_of(0, xT_hi, xT_lo, [0, 1, 2])
            transpose_projected()
            slabs_of(0, xT_hi, xT_lo, [3, 4])
            pe.wait_ge(conv_ready, 1)
            pe.wait_ge(small_loaded, 16 * 4)
            recurrent_gate(0)
            slabs_of(0, xT_hi, xT_lo, [5, 6])
            recurrent_gate(1)
            slabs_of(0, xT_hi, xT_lo, [7])
            for pair in (1, 2):
                start_projection()
                slabs_of(pair, xT_hi, xT_lo, [0])
                if pair == 1:
                    pe.wait_ge(cum_ready, 1)
                    free(0)
                    for t in range(TT):
                        mm = nc.tensor.transpose(aux[0][:, t * P:(t + 1) * P], sig[:, 3, t * P:(t + 1) * P], ident[:])
                    mm.then_inc(aux_ready[0], 1)
                slabs_of(pair, xT_hi, xT_lo, [1])
                if pair == 1:
                    for b in range(2):
                        free(b)
                        for hh in range(2):
                            h = 2 * b + hh
                            mm = nc.tensor.matmul(aux[b][:, hh * SEQ:(hh + 1) * SEQ],
                                                  ident[:, h:h + 1].to_broadcast([P, P]), sig[:, 3, 0:SEQ],
                                                  start=True, stop=True)
                        mm.then_inc(aux_ready[b], 1)
                slabs_of(pair, xT_hi, xT_lo, [2])
                transpose_projected()
                slabs_of(pair, xT_hi, xT_lo, [3, 4, 5, 6, 7])

            ready = Count(probs_ready)

            def scores(h):
                free(0)
                nc.tensor.matmul(aux[0][:, 0:P], qT[:, h, 0:P], kT[:, h, 0:P], start=True, stop=True)
                nc.tensor.matmul(aux[0][:, P:3 * P], qT[:, h, P:SEQ], kT[:, h, :],
                                 start=True, stop=True).then_inc(aux_ready[0], 1)

            def transpose_probs(h):
                pe.wait_ge(probs_ready, ready.next())
                free(1)
                p = logits[:, h % 2]
                for i in range(3):
                    mm = nc.tensor.transpose(aux[1][:, i * P:(i + 1) * P], p[:, i * P:(i + 1) * P], ident[:])
                mm.then_inc(aux_ready[1], 1)

            def mix(h):
                free(1)
                vh = slice(h * P, (h + 1) * P)
                nc.tensor.matmul(aux[1][:, 0:P], v_tok[:, 0, vh], probsT[:, 0:P], start=True, stop=True)
                nc.tensor.matmul(aux[1][:, P:SEQ], v_tok[:, 0, vh], probsT[:, P:SEQ], start=True, stop=False)
                nc.tensor.matmul(aux[1][:, P:SEQ], v_tok[:, 1, vh], probsT[:, SEQ:3 * P],
                                 start=False, stop=True).then_inc(aux_ready[1], 1)

            def attention_after(step, newer=1):
                h = step // 3
                if step == 0:
                    pe.wait_ge(aux_taken[1], job[1].value())
                if step == 4:
                    pe.wait_ge(u_taken, projected.value(newer))
                if step % 3 == 0 and 1 <= h <= HEADS:
                    transpose_probs(h - 1)
                if step % 3 == 1 and 1 <= h <= HEADS:
                    mix(h - 1)
                if step % 3 == 0 and h < HEADS:
                    scores(h)

            per = {slab: 3 * SLABS, projected: 3, ready: HEADS, job[0]: HEADS + 2, job[1]: 2 * HEADS + 2}
            with loop(pe, 2, per):
                for pair in range(3):
                    start_projection()
                    for s in range(SLABS):
                        slabs_of(pair, xT_hi, xT_lo, [s])
                        step = pair * SLABS + s
                        attention_after(step)
                        if step in (14, 18):
                            transpose_projected()

            merged = Count(merged_ready)
            mixed = Count(mix_taken)

            def merge_row(first):
                for g in range(4):
                    start_gate()
                    for s in range(SLABS):
                        slabs_of(g % 2, xT_hi, xT_lo, [s])
                        step = g * GATE_STEPS + s
                        if first:
                            attention_after(step, 0)
                        elif step == 2:
                            pe.wait_ge(merged_ready, merged.next())
                            transpose_stage()
                    if first and g == 0:
                        pe.wait_ge(u_taken, IN_GROUPS)
                    else:
                        pe.wait_ge(mix_taken, mixed.value())
                    if first:
                        if g == 1:
                            pe.wait_ge(branch_done, 1)
                        if g == 3:
                            pe.wait_ge(aux_taken[1], job[1].value())
                    mixed.next()
                    for s in range(MIX_SLABS):
                        products(2, oT_hi[:, g], oT_lo[:, g], [s], 0, MIX_SLABS - 1)
                        if first:
                            attention_after(g * GATE_STEPS + SLABS + s, 0)

            merge_row(True)
            mark["attention_done"] = job[1].n
            with loop(pe, CB - 1, {slab: ROW_STEPS, gated: 4, merged: 1, mixed: 4, job[0]: 1, job[1]: 1}):
                merge_row(False)

            for m in range(CB):
                start_group()
                if m == 0:
                    slabs_of(0, zT_hi, zT_lo, [0, 1, 2])
                    pe.wait_ge(merged_ready, merged.next())
                    transpose_stage()
                    slabs_of(0, zT_hi, zT_lo, [3, 4, 5])
                    for b in range(2):
                        pe.wait_ge(aux_taken[b], job[b].value())
                    slabs_of(0, zT_hi, zT_lo, [6, 7])
                elif m < CB - 1:
                    slabs_of(m % 2, zT_hi, zT_lo, range(SLABS))
                else:
                    slabs_of(m % 2, zT_hi, zT_lo, range(SLABS - LEAD))
                    rows_apart(m % 2, zT_hi, zT_lo, range(SLABS - LEAD, SLABS), SLABS - 1,
                               lambda: transpose_tile(0, 1))

            first_group(start_group, 1)
            mark["x1_transposed"] = [job[0].n, job[1].n]
            with loop(pe, QUARTERS, {slab: QUARTER_STEPS, groups: 2 * CB, job[0]: CB, job[1]: CB}) as q:
                for i in range(1, CB):
                    start_group()
                    slabs_of(i % 2, xT_hi, xT_lo, [0, 1, 2])
                    transpose_hidden(1)
                    slabs_of(i % 2, xT_hi, xT_lo, [3, 4, 5, 6, 7])
                for b in range(2):
                    pe.wait_ge(aux_taken[b], job[b].value())
                for i in range(CB):
                    start_group()
                    if i == 0:
                        slabs_of(0, zT_hi, zT_lo, [0, 1, 2])
                        transpose_hidden(1)
                        slabs_of(0, zT_hi, zT_lo, [3, 4, 5])
                        for b in range(2):
                            pe.wait_ge(aux_taken[b], job[b].value())
                        slabs_of(0, zT_hi, zT_lo, [6, 7])
                    elif i < CB - 1:
                        slabs_of(i % 2, zT_hi, zT_lo, range(SLABS))
                    else:
                        slabs_of(i % 2, zT_hi, zT_lo, range(SLABS - LEAD))
                        rows_apart(i % 2, zT_hi, zT_lo, range(SLABS - LEAD, SLABS), SLABS - 1)
                with pe.If(QUARTERS - 1 - q):
                    start_group()
                    slabs_of(0, xT_hi, xT_lo, range(SLABS))

        @block.scalar
        def _(act):
            slab = Count(hi_ready)
            job = [Count(aux_ready[0]), Count(aux_ready[1])]
            done = Count(act_done)
            std = Count(std_ready)
            hi_out = Count(evac_hi)

            def split(n):
                for _ in range(n):
                    slot = slab.n % RING
                    act.wait_ge(slab_loaded[slot], slab.scaled(16, RING) + 16)
                    if slab.n >= RING:
                        act.wait_ge(slab_used, slab.value(RING - 1))
                    nc.scalar.copy(w_hi[:, slot], w_raw[:, slot]).then_inc(hi_ready, 1)
                    slab.next()

            def settle():
                act.wait_ge(act_done, done.value())

            def did(ins):
                ins.then_inc(act_done, 1)
                done.next()

            def wait_job(b):
                act.wait_ge(aux_ready[b], job[b].next())

            def skip_job(b):
                job[b].next()

            def root(t):
                act.wait_ge(var_ready, std.next())
                nc.scalar.activation(rstd[:, t:t + 1], mean_var[:, t, 1:2], ACT.Sqrt).then_inc(std_ready, 1)

            normed = Count(normed_ready)

            def normed_pair(pair, gain, shift):
                b = pair % 2
                wait_job(b)
                if normed.n >= 2:
                    act.wait_ge(normed_ready, normed.value(1))
                normed.next()
                for kk in range(2):
                    k = 2 * pair + kk
                    ins = nc.scalar.activation(gate[:, b, kk * SEQ:(kk + 1) * SEQ], aux[b][:, kk * SEQ:(kk + 1) * SEQ],
                                               ACT.Identity, scale=params[:, gain + k:gain + k + 1],
                                               bias=params[:, shift + k:shift + k + 1])
                ins.then_inc(aux_taken[b], 1)

            def normed_quarter(t, b, gain, shift):
                wait_job(b)
                if normed.n >= 2:
                    act.wait_ge(normed_ready, normed.value(1))
                normed.next()
                for kk in range(4):
                    k = 4 * b + kk
                    ins = nc.scalar.activation(gate[:, b, kk * P:(kk + 1) * P], aux[b][:, kk * P:(kk + 1) * P],
                                               ACT.Identity, scale=params[:, gain + k:gain + k + 1],
                                               bias=params[:, shift + k:shift + k + 1])
                ins.then_inc(aux_taken[b], 1)

            def first_group(gain, shift):
                normed_quarter(1, 0, gain, shift)
                normed_quarter(1, 1, gain, shift)
                for s in range(SLABS):
                    split(1)
                    if 1 <= s <= SLABS // 2:
                        normed_pair(s + 3, gain, shift)

            for vec, at in PARAM_ROWS[:5]:
                load_params(act, vec, at)
            act.wait_ge(consts_ready, 1)
            nc.scalar.activation(first_root[:], ones[:, 0:1], ACT.Sqrt)
            for t in range(TT):
                root(t)
            split(1)
            skip_job(0)
            act.wait_ge(aux_taken[0], 1)
            normed_quarter(0, 0, LN_IN_G, LN_IN_B)
            split(1)
            normed_quarter(0, 1, LN_IN_G, LN_IN_B)
            split(2)
            act.dma_start(wf_raw[:], w_in[0][:, FORGET:FORGET + HEADS].rearrange("(k p) n -> p k n", p=P)).then_inc(small_loaded, 16)
            act.dma_start(w_ri[:, 0], w_r[0].rearrange("n c d -> c n d")).then_inc(small_loaded, 16)
            act.dma_start(w_ri[:, 1], w_i[0].rearrange("n c d -> c n d")).then_inc(small_loaded, 16)
            act.dma_start(b_forget_col[:], bass.AP(b_forget.tensor, b_forget.offset, [[0, P // HEADS], [1, HEADS], [1, 1]])
                          ).then_inc(small_loaded, 16)
            first_group(LN_IN_G, LN_IN_B)

            def to_rows(rows, pair):
                act.wait_ge(slab_used, slab.value(LEAD))
                nc.scalar.copy(rows[:, 0, :], acc[pair][0][:])
                nc.scalar.copy(rows[:, 1, :], acc[pair][1][:]).then_inc(u_taken, 1)

            def from_stage(to):
                for b in range(2):
                    wait_job(b)
                    nc.scalar.copy(to[:, 2 * b:2 * b + 2, :],
                                   aux[b][:].rearrange("p (k t) -> p k t", k=2)).then_inc(aux_taken[b], 1)

            def recurrent_gate(to, which):
                for b in range(2):
                    wait_job(b)
                    for hh in range(2):
                        n = 2 * b + hh
                        ins = nc.scalar.activation(to[:, n, :], aux[b][:, hh * SEQ:(hh + 1) * SEQ], ACT.Tanh,
                                                   scale=0.5, bias=lru_cols[:, which, n:n + 1])
                    ins.then_inc(aux_taken[b], 1)

            def decay(to, func, which, signal):
                for n in range(HEADS):
                    c = lru_cols[:, which, n:n + 1]
                    ins = nc.scalar.activation(to[:, n, :], lru[3][:, n, :], func, scale=c, bias=c)
                ins.then_inc(signal, 1)

            a, b_, c_, d_, e_, f_ = lru
            to_rows(stage, 0)
            act.wait_ge(small_loaded, 16 * 4)
            nc.scalar.copy(repeated(wf_hi[:]), wf_wide).then_inc(wf_hi_ready, 1)
            split(3)
            from_stage(a)
            split(1)
            skip_job(0)
            act.wait_ge(sig_in, 1)
            nc.scalar.activation(sig[:, 2, :], sig[:, 1, :], ACT.Exp).then_inc(sig_exp, 1)
            split(4)
            to_rows(stage, 1)
            split(3)
            from_stage(b_)
            split(2)
            act.wait_ge(lru_cols_ready, 1)
            recurrent_gate(d_, 0)
            split(2)
            recurrent_gate(e_, 1)
            act.wait_ge(aux_taken[1], job[1].value())
            skip_job(0)
            skip_job(0)
            skip_job(1)
            split(1)
            to_rows(stage, 0)
            split(1)
            decay(a, ACT.Exp, 2, decay_exp_ready)
            split(1)
            decay(f_, ACT.Tanh, 2, decay_tanh_ready)
            split(1)
            from_stage(qT)
            split(2)
            act.wait_ge(gated_x_ready, 1)
            decay(c_, ACT.Tanh, 3, decay_tanh_ready)
            split(3)
            to_rows(stage, 1)
            act.wait_ge(rest_ready, 1)
            nc.scalar.activation(f_[:], a[:], ACT.Sqrt, scale=-1.0).then_inc(root_ready, 1)
            split(3)
            from_stage(kT)
            split(1)
            act.wait_ge(gelu_in_ready, 1)
            nc.scalar.activation(f_[:], c_[:], ACT.Tanh, scale=GELU_C).then_inc(gelu_tanh_ready, 1)
            split(2)
            act.wait_ge(lru_out_ready, 1)
            nc.scalar.copy(oT_hi[:, 1], c_[:]).then_inc(evac_hi, 1)
            hi_out.next()
            split(2)
            to_rows(v_tok, 2)

            peaks = Count(peak_ready)
            stick = Count(stick_logits_ready)

            def probs_out(h):
                wait_job(1)
                nc.scalar.copy(probsT[:], aux[1][:, 0:3 * P]).then_inc(aux_taken[1], 1)

            def mixed_out(branch, h):
                wait_job(1)
                nc.scalar.copy(oT_hi[:, branch, h, :], aux[1][:, 0:SEQ]).then_inc(evac_hi, 1)
                hi_out.next()

            def softmax_exp(h):
                act.wait_ge(peak_ready, peaks.next())
                p = logits[:, h % 2]
                nc.scalar.activation(p[:, 0:P], p[:, 0:P], ACT.Exp, bias=neg_peak[:, 0:1], accum_out=total[:, 0:1])
                nc.scalar.activation(p[:, P:3 * P], p[:, P:3 * P], ACT.Exp, bias=neg_peak[:, 1:2],
                                     accum_out=total[:, 1:2]).then_inc(exp_ready, 1)

            def stick_log(h):
                wait_job(0)
                did(nc.scalar.activation(stick_l[:], aux[0][:, 0:3 * P], ACT.Abs, scale=SCALE))
                settle()
                did(nc.scalar.activation(stick_l[:], stick_l[:], ACT.Exp, scale=-1.0))
                settle()
                nc.scalar.activation(stick_l[:], stick_l[:], ACT.Ln, bias=1.0).then_inc(stick_log_ready, 1)

            def stick_exp(h):
                act.wait_ge(stick_logits_ready, stick.next())
                p = logits[:, h % 2]
                nc.scalar.activation(p, p, ACT.Exp).then_inc(probs_ready, 1)

            def attention_step(branch, step, stick_breaking):
                h = step // 3
                if step % 3 == 0:
                    if 1 <= h <= HEADS:
                        probs_out(h - 1)
                    if h < HEADS:
                        if stick_breaking:
                            stick_log(h)
                        else:
                            skip_job(0)
                if step % 3 == 1:
                    if 1 <= h <= HEADS:
                        mixed_out(branch, h - 1)
                    if h < HEADS and not stick_breaking:
                        softmax_exp(h)
                if step % 3 == 2 and h < HEADS and stick_breaking:
                    stick_exp(h)

            for branch in (0, 2):
                for step in range(3 * SLABS):
                    split(1)
                    attention_step(branch, step, branch == 2)
                    if step == 7:
                        to_rows(stage, 0)
                    if step == 14:
                        from_stage(qT)
                    if step == 15:
                        to_rows(stage, 1)
                    if step == 18:
                        from_stage(kT)
                    if step == 23:
                        to_rows(v_tok, 2)

            gates = Count(gate_in_ready)

            def halves_out(hi_to, b, scale=1.0):
                nc.scalar.activation(hi_to, aux[b][:].rearrange("p (k t) -> p k t", k=2), ACT.Copy,
                                     scale=scale).then_inc(evac_hi, 1)
                hi_out.next()

            def merge_row(first, n=None):
                for step in range(ROW_STEPS):
                    g, s = divmod(step, GATE_STEPS)
                    if not first and step == 3:
                        for b in range(2):
                            wait_job(b)
                    split(1)
                    if first:
                        attention_step(3, step, False)
                    elif step == 3:
                        for b in range(2):
                            k = n * (NC // P) + 2 * b
                            halves_out(zT_hi[:, bass.ds(k, 2), :], b, 0.5)
                    if s == SLABS:
                        act.wait_ge(gate_in_ready, gates.next())
                        nc.scalar.activation(gate[:], gate[:], ACT.Tanh, scale=0.5).then_inc(gate_ready, 1)

            merge_row(True)
            with loop(act, CB - 1, {slab: ROW_STEPS, job[0]: 1, job[1]: 1, hi_out: 2, gates: 4}) as n:
                merge_row(False, n)

            split(3)
            for b in range(2):
                wait_job(b)
                halves_out(zT_hi[:, (CB - 1) * (NC // P) + 2 * b:(CB - 1) * (NC // P) + 2 * b + 2, :], b, 0.5)
            split(CB * SLABS - LEAD - 3)

            root(0)
            split(2)
            normed_quarter(0, 0, LN1_G, LN1_B)
            normed_quarter(0, 1, LN1_G, LN1_B)
            split(2)
            root(1)
            relus = Count(relu_ready)

            def relu(pair):
                act.wait_ge(slab_used, slab.value(LEAD))
                nc.scalar.activation(stage[:, 0], acc[pair][0][:], ACT.Relu)
                nc.scalar.activation(stage[:, 1], acc[pair][1][:], ACT.Relu).then_inc(relu_ready, 1)
                relus.next()

            first_group(LN1_G, LN1_B)
            relu(0)

            with loop(act, QUARTERS, {slab: QUARTER_STEPS, job[0]: CB, job[1]: CB, hi_out: 2 * CB, relus: CB}) as q:
                for step in range(SLABS, QUARTER_STEPS - LEAD):
                    split(1)
                    i, s = divmod(step, SLABS)
                    if s == 2 and i <= CB:
                        for b in range(2):
                            wait_job(b)
                            k = (i - 1) * (NC // P) + 2 * b
                            halves_out(zT_hi[:, k:k + 2, :], b)
                    if s == SLABS - 1 and i < CB:
                        relu(i % 2)
                with act.If(QUARTERS - 1 - q):
                    split(LEAD + SLABS)
                    relu(0)
            for t, stretches in ((0, CB), (1, SHARED)):
                root(t)
                act.wait_ge(inv_ready, std.n)
                for m in range(stretches):
                    cols = slice(m * NC, (m + 1) * NC)
                    act.wait_ge(gained_ready, t * CB + m + 1)
                    nc.scalar.activation(x_tok[:, t, cols], x_tok[:, t, cols], ACT.Copy,
                                         scale=rstd[:, t:t + 1]).then_inc(scaled_ready, 1)

        @block.vector
        def _(dve):
            slab = Count(lo_ready)
            job = [Count(aux_ready[0]), Count(aux_ready[1])]
            done = Count(dve_done)
            std = Count(std_ready)
            hi_in = Count(evac_hi)
            acc_done = Count(acc_taken)
            v = nc.vector

            def split(n):
                for _ in range(n):
                    slot = slab.n % RING
                    dve.wait_ge(hi_ready, slab.next())
                    v.tensor_sub(w_lo[:, slot], w_raw[:, slot], w_hi[:, slot]).then_inc(lo_ready, 1)

            def did(ins):
                ins.then_inc(dve_done, 1)
                done.next()

            def settle():
                dve.wait_ge(dve_done, done.value())

            def chain(ins):
                did(ins)
                settle()

            def wait_job(b):
                dve.wait_ge(aux_ready[b], job[b].next())

            def skip_job(b):
                job[b].next()

            def statistics(t, m):
                did(v.bn_stats(bn[:, t, m], x_tok[:, t, m * NC:(m + 1) * NC]))

            def spread(t):
                settle()
                chain(v.bn_aggr(mean_var[:, t], bn[:, t].rearrange("p m s -> p (m s)")))
                v.tensor_scalar(mean_var[:, t, 1:2], mean_var[:, t, 1:2], EPS, None, ALU.add).then_inc(var_ready, 1)

            def invert_std(t):
                dve.wait_ge(std_ready, std.next())
                v.reciprocal(rstd[:, t:t + 1], rstd[:, t:t + 1]).then_inc(inv_ready, 1)
                dve.wait_ge(inv_ready, std.n)

            def normalise(t):
                invert_std(t)
                for cols in (slice(0, NC), slice(NC, D // 2)):
                    v.tensor_scalar(x_tok[:, t, cols], x_tok[:, t, cols], mean_var[:, t, 0:1], rstd[:, t:t + 1],
                                    ALU.subtract, ALU.mult).then_inc(xn_ready, 1)

            normed = Count(normed_ready)

            def normed_pair(pair):
                b = pair % 2
                skip_job(b)
                dve.wait_ge(aux_taken[b], job[b].value())
                ks = slice(2 * pair, 2 * pair + 2)
                full = gate[:, b].rearrange("p (k t) -> p k t", k=2)
                chain(v.tensor_copy(xT_hi[:, ks], full))
                v.tensor_sub(xT_lo[:, ks], full, xT_hi[:, ks]).then_inc(normed_ready, 1)

            def normed_quarter(t, b):
                skip_job(b)
                dve.wait_ge(aux_taken[b], job[b].value())
                ks, toks = slice(4 * b, 4 * b + 4), slice(t * P, (t + 1) * P)
                full = gate[:, b].rearrange("p (k t) -> p k t", k=4)
                chain(v.tensor_copy(xT_hi[:, ks, toks], full))
                v.tensor_sub(xT_lo[:, ks, toks], full, xT_hi[:, ks, toks]).then_inc(normed_ready, 1)

            def first_group():
                normed_quarter(1, 0)
                normed_quarter(1, 1)
                for s in range(SLABS):
                    if 1 <= s <= SLABS // 2:
                        normed_pair(s + 3)
                    split(1)

            did(v.memset(carry[:], ALPHA))
            for t in range(TT):
                for m in range(CB):
                    dve.wait_ge(x_loaded[t][m], 16)
                    statistics(t, m)
                    if t == 1 and m == 1:
                        normalise(0)
                if t == 1:
                    wait_job(0)
                    v.tensor_copy(params[:], aux[0][:, 0:PARAMS]).then_inc(aux_taken[0], 1)
                spread(t)
            normalise(1)
            split(1)
            normed_quarter(0, 0)
            split(1)
            normed_quarter(0, 1)
            split(2)
            first_group()

            a, b_, c_, d_, e_, f_ = lru
            arg, neg, ex, s1, s2, acc_ = [sig[:, i] for i in range(6)]
            dve.wait_ge(wf_hi_ready, 1)
            v.tensor_sub(repeated(wf_lo[:]), wf_wide, repeated(wf_hi[:])).then_inc(wf_ready, 1)
            did(v.tensor_scalar(lru_cols[:, 0], params[:, B_R:B_R + HEADS], 0.5, None, ALU.mult))
            did(v.tensor_scalar(lru_cols[:, 1], params[:, B_I:B_I + HEADS], 0.5, None, ALU.mult))
            split(3)

            skip_job(0)
            skip_job(1)
            dve.wait_ge(aux_taken[0], job[0].value())
            dve.wait_ge(aux_taken[1], job[1].value())
            for n in range(HEADS):
                tap = [params[:, CONV_W + j * HEADS + n:CONV_W + j * HEADS + n + 1] for j in range(CONV)]
                chain(v.tensor_scalar(c_[:, n], a[:, n], tap[CONV - 1], params[:, CONV_B + n:CONV_B + n + 1],
                                      ALU.mult, ALU.add))
                for j in reversed(range(CONV - 1)):
                    lag = CONV - 1 - j
                    ins = v.scalar_tensor_tensor(c_[:, n, lag:], a[:, n, 0:SEQ - lag], tap[j], c_[:, n, lag:],
                                                 ALU.mult, ALU.add)
                    if j or n < HEADS - 1:
                        chain(ins)
                if n == 0:
                    wait_job(0)
                    did(v.tensor_copy(arg[:, SEQ:], params[:, LAM:LAM + HEADS]))
                    v.tensor_scalar(arg[:, 0:SEQ], aux[0][:, 0:SEQ], b_forget_col[:], None, ALU.add).then_inc(aux_taken[0], 1)
                    dve.wait_ge(aux_taken[0], job[0].value())
                    v.scalar_tensor_tensor(neg, arg, -1.0, arg, ALU.mult, ALU.min).then_inc(sig_in, 1)
                if n < HEADS - 1:
                    split(1)
            ins.then_inc(conv_ready, 1)
            split(1)

            dve.wait_ge(sig_exp, 1)
            chain(v.tensor_scalar(s1, ex, 2.0, None, ALU.add))
            chain(v.reciprocal(s1, s1))
            split(1)
            chain(v.tensor_tensor(s1, s1, ex, ALU.mult))
            chain(v.tensor_tensor(s2, s1, s1, ALU.mult))
            chain(v.tensor_scalar(acc_, s2, 1.0 / 15, None, ALU.mult))
            split(1)
            for odd in (13, 11, 9, 7, 5, 3):
                chain(v.scalar_tensor_tensor(acc_, acc_, 1.0 / odd, s2, ALU.add, ALU.mult))
                if odd == 9:
                    split(1)
            split(1)
            chain(v.scalar_tensor_tensor(acc_, acc_, 1.0, s1, ALU.add, ALU.mult))
            chain(v.tensor_scalar(neg, arg, 0.0, None, ALU.min))
            chain(v.scalar_tensor_tensor(acc_, acc_, -2.0, neg, ALU.mult, ALU.add))
            did(v.tensor_scalar(lru_cols[:, 2], acc_[:, SEQ:], 4.0, None, ALU.mult))
            v.tensor_scalar(lru_cols[:, 3], acc_[:, SEQ:], 2.0, None, ALU.mult).then_inc(lru_cols_ready, 1)
            split(1)
            v.tensor_tensor_scan(sig[:, 3, 0:SEQ], ones[:], acc_[:, 0:SEQ], 0.0, ALU.mult, ALU.add).then_inc(cum_ready, 1)

            for _ in range(2):
                skip_job(0)
                skip_job(1)
            split(3)
            skip_job(0)
            skip_job(1)
            for b in range(2):
                dve.wait_ge(aux_taken[b], job[b].value())
            v.scalar_tensor_tensor(e_[:], e_[:], 1.0, c_[:], ALU.add, ALU.mult).then_inc(gated_x_ready, 1)
            split(2)

            wait_job(0)
            v.tensor_copy(cum_q[:], aux[0][:, 0:SEQ].rearrange("p (t r) -> p t r", t=TT)[:, :, 0:HEADS]
                          ).then_inc(aux_taken[0], 1)
            dve.wait_ge(aux_taken[0], job[0].value())
            for b in range(2):
                wait_job(b)
                for hh in range(2):
                    h = 2 * b + hh
                    sums = aux[b][:, hh * SEQ:(hh + 1) * SEQ]
                    did(v.tensor_scalar(fox_bias[:, h, 0:P], sums[:, 0:P], -1.0, cum_q[:, 0, h:h + 1], ALU.mult, ALU.add))
                    ins = v.tensor_scalar(fox_bias[:, h, P:3 * P], sums, -1.0, cum_q[:, 1, h:h + 1], ALU.mult, ALU.add)
                    if hh == 0:
                        did(ins)
                ins.then_inc(aux_taken[b], 1)
                dve.wait_ge(aux_taken[b], job[b].value())
            split(3)
            settle()
            diagonal = fox_bias[:].rearrange("p h (c k) -> p h c k", k=P)[:, :, 0::2, :]
            chain(v.tensor_tensor(diagonal, diagonal,
                                  causal_add[:].unsqueeze(1).unsqueeze(1).to_broadcast([P, HEADS, 2, P]), ALU.add))
            split(1)

            dve.wait_ge(gated_x_ready, 1)
            dve.wait_ge(decay_exp_ready, 1)
            dve.wait_ge(decay_tanh_ready, 2)
            chain(v.scalar_tensor_tensor(c_[:], a[:], 1.0, c_[:], ALU.add, ALU.mult))
            chain(v.tensor_scalar(d_[:], c_[:], 1.0, None, ALU.add))
            split(1)
            chain(v.tensor_tensor(a[:], d_[:], d_[:], ALU.mult))
            v.scalar_tensor_tensor(a[:], a[:], 1.0, f_[:], ALU.add, ALU.mult).then_inc(rest_ready, 1)
            split(1)
            chain(v.tensor_tensor(c_[:], b_[:], b_[:], ALU.mult))
            split(1)
            chain(v.tensor_scalar(c_[:], c_[:], 0.044715, 1.0, ALU.mult, ALU.add))
            chain(v.tensor_tensor(c_[:], c_[:], b_[:], ALU.mult))
            split(1)
            dve.wait_ge(root_ready, 1)
            v.scalar_tensor_tensor(e_[:], e_[:], 0.5, f_[:], ALU.mult, ALU.mult).then_inc(gelu_in_ready, 1)
            dve.wait_ge(gelu_in_ready, 1)
            dve.wait_ge(rest_ready, 1)
            split(1)
            for n in range(HEADS):
                did(v.tensor_tensor_scan(a[:, n], d_[:, n], e_[:, n], 0.0, ALU.mult, ALU.add))
                if n == 1:
                    split(1)
            settle()
            split(1)
            dve.wait_ge(gelu_tanh_ready, 1)
            chain(v.scalar_tensor_tensor(c_[:], f_[:], 1.0, b_[:], ALU.add, ALU.mult))
            v.scalar_tensor_tensor(c_[:], c_[:], 0.5, a[:], ALU.mult, ALU.mult).then_inc(lru_out_ready, 1)
            split(2)
            dve.wait_ge(lru_out_ready, 1)
            dve.wait_ge(evac_hi, hi_in.next())
            v.tensor_sub(oT_lo[:, 1], c_[:], oT_hi[:, 1]).then_inc(branch_done, 1)
            split(2)
            for _ in range(2):
                skip_job(0)
                skip_job(1)

            exps = Count(exp_ready)
            logs = Count(stick_log_ready)

            def softmax_logits(h, bias0, bias1):
                wait_job(0)
                p = logits[:, h % 2]
                did(v.scalar_tensor_tensor(p[:, 0:P], aux[0][:, 0:P], SCALE, bias0, ALU.mult, ALU.add))
                v.scalar_tensor_tensor(p[:, P:3 * P], aux[0][:, P:3 * P], SCALE, bias1,
                                       ALU.mult, ALU.add).then_inc(aux_taken[0], 1)
                settle()
                dve.wait_ge(aux_taken[0], job[0].value())
                did(v.tensor_reduce(peak[:, 0:1], p[:, 0:P], AX.X, ALU.max))
                chain(v.tensor_reduce(peak[:, 1:2], p[:, P:3 * P], AX.X, ALU.max))
                v.tensor_scalar(neg_peak[:], peak[:], -1.0, None, ALU.mult).then_inc(peak_ready, 1)

            def softmax_scale(h):
                dve.wait_ge(exp_ready, exps.next())
                p = logits[:, h % 2]
                chain(v.reciprocal(inv_total[:], total[:]))
                did(v.tensor_scalar(p[:, 0:P], p[:, 0:P], inv_total[:, 0:1], None, ALU.mult))
                v.tensor_scalar(p[:, P:3 * P], p[:, P:3 * P], inv_total[:, 1:2], None, ALU.mult).then_inc(probs_ready, 1)

            def stick_relu(h):
                wait_job(0)
                dve.wait_ge(stick_log_ready, logs.next())
                chain(v.tensor_scalar(stick_b[:], aux[0][:, 0:3 * P], SCALE, 0.0, ALU.mult, ALU.max))

            def stick_logits(h):
                chain(v.scalar_tensor_tensor(stick_b[:], stick_b[:], -1.0, stick_l[:], ALU.mult, ALU.subtract))
                diag = stick_b[:].rearrange("p (c k) -> p c k", k=P)[:, 0::2, :]
                chain(v.tensor_tensor(diag, diag, strict_mul[:].unsqueeze(1).to_broadcast([P, 2, P]), ALU.mult))
                did(v.tensor_tensor_scan(stick_c[:, P - 1::-1], ones[:, 0:P], stick_b[:, P - 1::-1], 0.0, ALU.mult, ALU.add))
                chain(v.tensor_tensor_scan(stick_c[:, 3 * P - 1:P - 1:-1], ones[:], stick_b[:, 3 * P - 1:P - 1:-1],
                                           0.0, ALU.mult, ALU.add))
                p = logits[:, h % 2]
                v.scalar_tensor_tensor(p, aux[0][:, 0:3 * P], SCALE, stick_c[:], ALU.mult, ALU.add).then_inc(aux_taken[0], 1)
                dve.wait_ge(aux_taken[0], job[0].value())
                diag = p.rearrange("p (c k) -> p c k", k=P)[:, 0::2, :]
                v.tensor_tensor(diag, diag, strict_add[:].unsqueeze(1).to_broadcast([P, 2, P]),
                                ALU.add).then_inc(stick_logits_ready, 1)

            def mixed_out(branch, h):
                wait_job(1)
                dve.wait_ge(evac_hi, hi_in.next())
                v.tensor_sub(oT_lo[:, branch, h, :], aux[1][:, 0:SEQ], oT_hi[:, branch, h, :]).then_inc(aux_taken[1], 1)

            def attention_step(branch, step):
                h = step // 3
                if step % 3 == 0 and 1 <= h <= HEADS:
                    skip_job(1)
                if step % 3 == 1 and 1 <= h <= HEADS:
                    mixed_out(branch, h - 1)
                if h >= HEADS:
                    return
                if branch == 2:
                    if step % 3 == 1:
                        stick_relu(h)
                        stick_logits(h)
                else:
                    if step % 3 == 0 and branch == 0:
                        softmax_logits(h, fox_bias[:, h, 0:P], fox_bias[:, h, P:3 * P])
                    if step % 3 == 0 and branch == 3:
                        softmax_logits(h, band_bias[:, h, P - 1::-1], band_bias[:, h, SEQ - 1::-1])
                    if step % 3 == 2:
                        softmax_scale(h)

            for branch in (0, 2):
                for step in range(3 * SLABS):
                    attention_step(branch, step)
                    split(1)
                    if step in (14, 18):
                        skip_job(0)
                        skip_job(1)
                    if branch == 0 and step == 11:
                        v.memset(band_bias[0:CHUNK, :, 0:CHUNK], MASKED).then_inc(rel_mask_ready, 1)

            gates = Count(gate_ready)
            biases = Count(gate_bias_loaded[0])

            def merge_row(first, n=None):
                for step in range(ROW_STEPS):
                    g, s = divmod(step, GATE_STEPS)
                    if first:
                        if step == 0:
                            dve.wait_ge(rel_loaded, 32)
                            dve.wait_ge(rel_mask_ready, 1)
                        attention_step(3, step)
                    elif step == 2:
                        for b in range(2):
                            wait_job(b)
                            dve.wait_ge(evac_hi, hi_in.next())
                            k = n * (NC // P) + 2 * b
                            v.scalar_tensor_tensor(zT_lo[:, bass.ds(k, 2), :], aux[b][:].rearrange("p (k t) -> p k t", k=2),
                                                   0.5, zT_hi[:, bass.ds(k, 2), :], ALU.mult, ALU.subtract).then_inc(aux_taken[b], 1)
                    split(1)
                    if s == SLABS - 1:
                        dve.wait_ge(slab_used, slab.value(LEAD))
                        dve.wait_ge(gate_bias_loaded[g % 2], biases.scaled(16, 2) + 16)
                        biases.next()
                        v.tensor_tensor(gate[:, 0], acc[g % 2][0][:], b_gate_rows[:, g % 2], ALU.add)
                        v.tensor_tensor(gate[:, 1], acc[g % 2][1][:], b_gate_rows[:, g % 2], ALU.add).then_inc(gate_in_ready, 1)
                    if s == GATE_STEPS - 1:
                        dve.wait_ge(slab_used, slab.value(LEAD))
                        dve.wait_ge(gate_ready, gates.next())
                        for t in range(TT):
                            to = stage if g == 0 else gate
                            ins = v.scalar_tensor_tensor(to[:, t], gate[:, t], 1.0, acc[2][t][:], ALU.add, ALU.mult)
                        ins.then_inc(mix_taken, 1)
                        mixed.next()
                        if g:
                            dve.wait_ge(mix_taken, mixed.value())
                            ins = v.tensor_tensor(stage[:], stage[:], gate[:], ALU.add)
                            if g == 3:
                                ins.then_inc(merged_ready, 1)
                            else:
                                did(ins)
                                settle()

            mixed = Count(mix_taken)
            merge_row(True)
            with loop(dve, CB - 1, {slab: ROW_STEPS, job[0]: 1, job[1]: 1, hi_in: 2, gates: 4, biases: 4,
                                    mixed: 4, done: 2}) as n:
                merge_row(False, n)

            split(3)
            for b in range(2):
                wait_job(b)
                dve.wait_ge(evac_hi, hi_in.next())
                k = (CB - 1) * (NC // P) + 2 * b
                v.scalar_tensor_tensor(zT_lo[:, k:k + 2, :], aux[b][:].rearrange("p (k t) -> p k t", k=2),
                                       0.5, zT_hi[:, k:k + 2, :], ALU.mult, ALU.subtract).then_inc(aux_taken[b], 1)
            def accumulate(t, m, factor):
                cols = slice(m * NC, (m + 1) * NC)
                ins = v.scalar_tensor_tensor(x_tok[:, t, cols], x_tok[:, t, cols], factor, acc[m % 2][t][:], ALU.mult, ALU.add)
                if t == 0:
                    chain(ins)
                else:
                    ins.then_inc(acc_taken, 1)
                    dve.wait_ge(acc_taken, acc_done.next())
                statistics(t, m)

            rows0 = Count(row0_ready)
            dve.wait_ge(residual_ready, 1)
            for m in range(CB - 1):
                split(SLABS - 3 if m == 0 else SLABS)
                dve.wait_ge(slab_used, slab.value(LEAD))
                for t in range(TT):
                    accumulate(t, m, ALPHA)
            split(LEAD)
            dve.wait_ge(row0_ready, rows0.next())
            accumulate(0, CB - 1, ALPHA)
            spread(0)
            normalise(0)
            split(2)
            normed_quarter(0, 0)
            dve.wait_ge(slab_used, slab.value(2))
            accumulate(1, CB - 1, ALPHA)
            spread(1)
            normed_quarter(0, 1)
            normalise(1)
            split(2)
            relus = Count(relu_ready)

            def hidden(pair):
                dve.wait_ge(relu_ready, relus.next())
                for t in range(TT):
                    ins = v.tensor_tensor(stage[:, t], acc[pair][t][:], stage[:, t], ALU.mult)
                ins.then_inc(acc_taken, 1)
                acc_done.next()

            first_group()
            hidden(0)

            with loop(dve, QUARTERS, {relus: CB, slab: QUARTER_STEPS, job[0]: CB, job[1]: CB, hi_in: 2 * CB,
                                      acc_done: 2 * CB, rows0: 1, done: 3 * CB + 1}) as q:
                for step in range(SLABS, QUARTER_STEPS - LEAD):
                    i, s = divmod(step, SLABS)
                    if s == 2 and i <= CB:
                        for b in range(2):
                            wait_job(b)
                            dve.wait_ge(evac_hi, hi_in.next())
                            k = (i - 1) * (NC // P) + 2 * b
                            v.tensor_sub(zT_lo[:, k:k + 2, :], aux[b][:].rearrange("p (k t) -> p k t", k=2),
                                         zT_hi[:, k:k + 2, :]).then_inc(aux_taken[b], 1)
                    split(1)
                    if s == SLABS - 1:
                        if i < CB:
                            hidden(i % 2)
                        else:
                            dve.wait_ge(slab_used, slab.value(LEAD))
                            if i == CB:
                                dve.wait_ge(residual_ready, 2)
                            for t in range(TT):
                                accumulate(t, i - CB, carry[:])
                before = {c: c.n for c in (relus, slab, acc_done, rows0, done)}
                with dve.If(QUARTERS - 1 - q):
                    dve.wait_ge(row0_ready, rows0.next())
                    accumulate(0, CB - 1, carry[:])
                    split(LEAD - 1)
                    dve.wait_ge(slab_used, slab.value(LEAD - 1))
                    accumulate(1, CB - 1, carry[:])
                    did(v.memset(carry[:], 1.0))
                    split(SLABS + 1)
                    hidden(0)
                left_out = {c: c.n - n for c, n in before.items()}
            for c, n in left_out.items():
                c.n -= n

            def gained(t, m):
                cols = slice(m * NC, (m + 1) * NC)
                return v.scalar_tensor_tensor(x_tok[:, t, cols], x_tok[:, t, cols], mean_var[:, t, 0:1],
                                              norm_rows[:, 0, cols], ALU.subtract, ALU.mult)

            dve.wait_ge(row0_ready, rows0.next())
            accumulate(0, CB - 1, carry[:])
            spread(0)
            invert_std(0)
            dve.wait_ge(norm_loaded, 96)
            for m in range(CB):
                gained(0, m).then_inc(gained_ready, 1)
            dve.wait_ge(slab_used, slab.value())
            accumulate(1, CB - 1, carry[:])
            spread(1)
            invert_std(1)
            for m in range(CB):
                if m < SHARED:
                    gained(1, m).then_inc(gained_ready, 1)
                else:
                    did(gained(1, m))
            settle()
            for m in range(SHARED, CB):
                cols = slice(m * NC, (m + 1) * NC)
                v.scalar_tensor_tensor(x_tok[:, 1, cols], x_tok[:, 1, cols], rstd[:, 1:2],
                                       norm_rows[:, 1, cols], ALU.mult, ALU.add).then_inc(dve_rows_ready, 1)

        @block.gpsimd
        def _(pool):
            g = nc.gpsimd
            for tile, value in ((ident, 0.0), (ones, 1.0), (causal_add, 0.0), (strict_add, 0.0),
                                (strict_mul, 1.0)):
                ins = g.memset(tile[:], value)
            ins.then_inc(pool_done, 1)
            pool.wait_ge(pool_done, 1)
            g.affine_select(out=ident[:], in_=ident[:], compare_op=ALU.not_equal, fill=1.0, base=0,
                            pattern=[[-1, P]], channel_multiplier=1)
            g.affine_select(out=causal_add[:], in_=causal_add[:], compare_op=ALU.is_ge, fill=MASKED, base=0,
                            pattern=[[-1, P]], channel_multiplier=1)
            g.affine_select(out=strict_add[:], in_=strict_add[:], compare_op=ALU.is_ge, fill=MASKED, base=-1,
                            pattern=[[-1, P]], channel_multiplier=1)
            g.affine_select(out=strict_mul[:], in_=strict_mul[:], compare_op=ALU.is_ge, fill=0.0, base=-1,
                            pattern=[[-1, P]], channel_multiplier=1).then_inc(consts_ready, 1)
            def normalise_rest(norm):
                for t in range(TT):
                    pool.wait_ge(inv_ready, TT * norm + t + 1)
                    g.tensor_scalar(x_tok[:, t, D // 2:], x_tok[:, t, D // 2:], mean_var[:, t, 0:1], rstd[:, t:t + 1],
                                    ALU.subtract, ALU.mult).then_inc(xn_rest_ready, 1)

            normalise_rest(0)
            pool.wait_ge(norm_loaded, 32)
            for t in range(TT):
                ins = g.tensor_tensor(x_tok[:, t], x_tok[:, t], norm_rows[:, 0], ALU.mult)
            ins.then_inc(pool_done, 1)
            pool.wait_ge(pool_done, 2)
            for t in range(TT):
                ins = g.tensor_tensor(x_tok[:, t], x_tok[:, t], norm_rows[:, 1], ALU.add)
            ins.then_inc(residual_ready, 1)
            normalise_rest(1)
            pool.wait_ge(norm_loaded, 64)
            for b in range(2):
                pool.wait_ge(aux_ready[b], mark["x1_transposed"][b])
            for t in range(TT):
                ins = g.tensor_tensor(x_tok[:, t], x_tok[:, t], norm_rows[:, 0], ALU.mult)
            ins.then_inc(pool_done, 1)
            pool.wait_ge(pool_done, 3)
            for t in range(TT):
                ins = g.tensor_tensor(x_tok[:, t], x_tok[:, t], norm_rows[:, 1], ALU.add)
            ins.then_inc(residual_ready, 1)
            for n in range(CB + SHARED):
                t, m = divmod(n, CB)
                cols = slice(m * NC, (m + 1) * NC)
                pool.wait_ge(scaled_ready, n + 1)
                g.tensor_tensor(x_tok[:, t, cols], x_tok[:, t, cols], norm_rows[:, 1, cols],
                                ALU.add).then_inc(pool_rows_ready, 1)

        @block.sync
        def _(sp):
            slab = Count(lo_ready)
            biases = Count(gate_in_ready)

            def load_slab(view):
                slot = slab.n % RING
                if slab.n >= RING:
                    sp.wait_ge(lo_ready, slab.value(RING - 1))
                sp.dma_start(w_raw[:, slot], view.rearrange("(k p) n -> p k n", p=P)).then_inc(slab_loaded[slot], 16)
                slab.next()

            def load_group(w, col, slabs=SLABS):
                for s in range(slabs):
                    load_slab(w[s * SLAB_K * P:(s + 1) * SLAB_K * P, bass.ds(col, NC)])

            def load_norm(gain, shift):
                sp.dma_start(norm_rows[:, 0], gain.partition_broadcast(P)).then_inc(norm_loaded, 16)
                sp.dma_start(norm_rows[:, 1], shift.partition_broadcast(P)).then_inc(norm_loaded, 16)

            for t in range(TT):
                for m in range(CB):
                    cols = slice(m * NC, (m + 1) * NC)
                    sp.dma_start(x_tok[:, t, cols], x[0, t * P:(t + 1) * P, cols]).then_inc(x_loaded[t][m], 16)
            for vec, at in PARAM_ROWS[5:]:
                load_params(sp, vec, at)
            for j in range(2):
                load_group(w_in[0], LRU + j * NC)
            with loop(sp, 3, {slab: SLABS}) as j:
                load_group(w_in[0], FOX + j * NC)
            with loop(sp, 6, {slab: SLABS}) as j:
                load_group(w_in[0], STICK + j * NC)
            rel = rel_bias[0]
            sp.wait_ge(rel_mask_ready, 1)
            for half, first in ((0, CHUNK), (1, 0)):
                src = bass.AP(rel.tensor, rel.offset, [[1, CHUNK], [REL, HEADS], [1, SEQ - first]])
                sp.dma_start(band_bias[half * CHUNK:(half + 1) * CHUNK, :, first:], src).then_inc(rel_loaded, 16)

            def load_merge_row(col, first):
                for g in range(4):
                    if not first or g >= 2:
                        sp.wait_ge(gate_in_ready, biases.value(1))
                    sp.dma_start(b_gate_rows[:, g % 2], b_gate[0][g, bass.ds(col, NC)].partition_broadcast(P)
                                 ).then_inc(gate_bias_loaded[g % 2], 16)
                    biases.next()
                    load_group(w_gate[0][g], col)
                    load_group(w_branch[0][g], col, MIX_SLABS)

            load_merge_row(0, True)
            sp.wait_ge(aux_taken[1], mark["attention_done"])
            load_norm(ln_in_g, ln_in_b)
            with loop(sp, CB - 1, {slab: ROW_STEPS, biases: 4}) as n:
                load_merge_row(n * NC + NC, False)
            sp.wait_ge(residual_ready, 1)
            load_norm(ln1_g[0], ln1_b[0])
            with loop(sp, CB, {slab: SLABS}) as m:
                load_group(w_out[0], m * NC)
            with loop(sp, QUARTERS, {slab: QUARTER_STEPS}) as q:
                with loop(sp, CB, {slab: SLABS}) as i:
                    load_group(w_ff1[0], q * D + i * NC)
                with loop(sp, CB, {slab: SLABS}) as m:
                    for s in range(SLABS):
                        load_slab(w_ff2[0][bass.ds(q * D + s * SLAB_K * P, SLAB_K * P), bass.ds(m * NC, NC)])
            sp.wait_ge(residual_ready, 2)
            load_norm(ln2_g[0], ln2_b[0])
            def store(t, m):
                cols = slice(m * NC, (m + 1) * NC)
                sp.dma_start(out[0, t * P:(t + 1) * P, cols], x_tok[:, t, cols]).then_inc(out_stored, 16)

            for n in range(CB):
                sp.wait_ge(pool_rows_ready, n + 1)
                store(0, n)
            for n in range(SHARED):
                sp.wait_ge(pool_rows_ready, CB + n + 1)
                store(1, n)
                sp.wait_ge(dve_rows_ready, n + 1)
                store(1, SHARED + n)
            sp.wait_ge(out_stored, 16 * TT * CB)


INPUTS = ["x", "ln_in_g", "ln_in_b", "w_in", "b_forget", "conv_w", "conv_b", "w_r", "b_r", "w_i", "b_i", "lru_lambda",
          "rel_bias", "w_branch", "w_gate", "b_gate", "w_out", "ln1_g", "ln1_b", "w_ff1", "w_ff2", "ln2_g", "ln2_b"]


def kernel(**inputs):
    import numpy as np
    import concourse.bacc as bacc
    from concourse.bass_utils import run_bass_kernel_spmd

    nc = bacc.Bacc("TRN2", target_bir_lowering=False, num_devices=1)
    arrays, args = {}, []
    for name in INPUTS:
        a = np.ascontiguousarray(inputs[name])
        arrays[f"in_{name}"] = a
        args.append(nc.dram_tensor(f"in_{name}", a.shape, mybir.dt.from_np(a.dtype), kind="ExternalInput").ap())
    args.append(nc.dram_tensor("out_x", (1, SEQ, D), F32, kind="ExternalOutput").ap())
    build(nc, *args)
    return run_bass_kernel_spmd(nc, [arrays], core_ids=[0]).results[0]["out_x"]
```
